# Optimizing a Trainium2 kernel written in Bass

```python
import math
import jax, jax.numpy as jnp
from jax import lax
import numpy as np

D_MODEL = 1024
BATCH = 1
SEQ = 512
DEPTH = 2

GRID_W = 64
CTX_LEN = 256
N_MIXERS = 3
RMS_EPS = 1e-6
CONV_WIDTH = 3
HGRN_HEADS = 8
HGRN_HEAD_DIM = D_MODEL // HGRN_HEADS
HGRN_CHUNK = 32
S5_GROUP = 16
S5_GROUPS = D_MODEL // S5_GROUP
S5_STATE = 64
S5_MIN_STEP = 1e-3
S5_MAX_STEP = 1e-1
S5_CLIP = 1e-4
PEER_HEADS = 8
PEER_NKEYS = 128
PEER_EXPERTS = PEER_NKEYS * PEER_NKEYS
PEER_QDIM = 256
PEER_HALF = PEER_QDIM // 2
PEER_TOPK = 16
PEER_BLOCK = 128
PEER_V_SCALE = 0.5

kernel_name = 'hybrid_conv_hgrn2_s5_peer_dit'

def _n_layers_of(kind):
    return len(range(kind, DEPTH, N_MIXERS))

def rms_norm(x, g):
    xf = x.astype(jnp.float32)
    y = xf * lax.rsqrt(jnp.mean(xf * xf, axis=-1, keepdims=True) + RMS_EPS)
    return (y * g.astype(jnp.float32)).astype(x.dtype)

def adaln(cond, w, b):
    return jnp.split(jax.nn.silu(cond) @ w + b, 6, axis=-1)

def modulate(h, shift, scale):
    return h * (1 + scale) + shift

def centred_conv3(z, k):
    pad = [(0, 0)] * (z.ndim - 2) + [(1, 1), (0, 0)]
    zp = jnp.pad(z, pad)
    return zp[..., :-2, :] * k[0] + zp[..., 1:-1, :] * k[1] + zp[..., 2:, :] * k[2]

def short_conv_mixer(h, w_in, k, w_out, rows):
    gate_b, gate_c, v = jnp.split(h @ w_in, 3, axis=-1)
    z = gate_c * v
    if rows is None:
        zc = centred_conv3(z, k)
    else:
        bn, t, ch = z.shape
        zc = centred_conv3(z.reshape(bn, rows, GRID_W, ch), k).reshape(bn, t, ch)
    return (gate_b * zc) @ w_out

def gla_chunk_scan(q, k, v, g, s0):
    bn, t, nh, dk = q.shape
    L = HGRN_CHUNK
    n = t // L
    def chunks(a):
        return a.reshape(bn, n, L, nh, a.shape[-1]).transpose(1, 0, 2, 3, 4)
    q, k, v, g = chunks(q), chunks(k), chunks(v), chunks(g)
    b = jnp.cumsum(g, axis=2)
    b_mid = b[:, :, L // 2:L // 2 + 1]
    scores = jnp.einsum('nblhk,nbmhk->nbhlm', q * jnp.exp(b - b_mid), k * jnp.exp(b_mid - b))
    tri = jnp.tril(jnp.ones((L, L), dtype=bool))
    o_intra = jnp.einsum('nbhlm,nbmhv->nblhv', jnp.where(tri, scores, 0.0), v)
    q_dec = q * jnp.exp(b)
    k_dec = k * jnp.exp(b[:, :, -1:] - b)
    decay = jnp.exp(b[:, :, -1])

    def step(s, xs):
        qd, kd, vv, dc = xs
        o = jnp.einsum('blhk,bhkv->blhv', qd, s)
        s = dc[..., None] * s + jnp.einsum('blhk,blhv->bhkv', kd, vv)
        return s, o

    s_last, o_inter = lax.scan(step, s0, (q_dec, k_dec, v, decay))
    o = (o_intra + o_inter).transpose(1, 0, 2, 3, 4).reshape(bn, t, nh, v.shape[-1])
    return o, s_last

def hgrn2_mixer(hc, hx, w_in, lb, norm_g, w_out):
    def project(h):
        bn, t, _ = h.shape
        heads = lambda a: a.astype(jnp.float32).reshape(bn, t, HGRN_HEADS, HGRN_HEAD_DIM)
        q, i, zf_fwd, zf_bwd, zg = jnp.split(h @ w_in, 5, axis=-1)
        dirs = []
        for d, zf in enumerate((zf_fwd, zf_bwd)):
            f = heads(lb[d] + (1.0 - lb[d]) * jax.nn.sigmoid(zf.astype(jnp.float32)))
            dirs.append((1.0 - f, jnp.log(f)))
        return heads(jax.nn.silu(q)), heads(i), dirs, zg

    qc, vc, dc, zgc = project(hc)
    qx, vx, dx, zgx = project(hx)
    s0 = jnp.zeros((hc.shape[0], HGRN_HEADS, HGRN_HEAD_DIM, HGRN_HEAD_DIM), jnp.float32)
    fl = lambda a: jnp.flip(a, axis=1)
    oc_f, sc_f = gla_chunk_scan(qc, dc[0][0], vc, dc[0][1], s0)
    ox_f, _ = gla_chunk_scan(qx, dx[0][0], vx, dx[0][1], sc_f)
    oc_b, sc_b = gla_chunk_scan(fl(qc), fl(dc[1][0]), fl(vc), fl(dc[1][1]), s0)
    ox_b, _ = gla_chunk_scan(fl(qx), fl(dx[1][0]), fl(vx), fl(dx[1][1]), sc_b)

    def readout(o, zg):
        bn, t = o.shape[:2]
        on = rms_norm(o, norm_g.reshape(HGRN_HEADS, HGRN_HEAD_DIM)).reshape(bn, t, D_MODEL)
        return (on.astype(zg.dtype) * jax.nn.silu(zg)) @ w_out

    return readout(oc_f + fl(oc_b), zgc), readout(ox_f + fl(ox_b), zgx)

def s5_discretise(lam_re, lam_im, log_step, b_re, b_im):
    step = jnp.exp(log_step.astype(jnp.float32))[:, None]
    lr = jnp.minimum(lam_re.astype(jnp.float32), -S5_CLIP)
    li = lam_im.astype(jnp.float32)
    ar, ai = step * lr, step * li
    mag = jnp.exp(ar)
    abar_r, abar_i = mag * jnp.cos(ai), mag * jnp.sin(ai)
    den = lr * lr + li * li
    fr = ((abar_r - 1.0) * lr + abar_i * li) / den
    fi = (abar_i * lr - (abar_r - 1.0) * li) / den
    br, bi = b_re.astype(jnp.float32), b_im.astype(jnp.float32)
    bbar_r = fr[..., None] * br - fi[..., None] * bi
    bbar_i = fr[..., None] * bi + fi[..., None] * br
    return (ar, ai), (abar_r, abar_i), (bbar_r, bbar_i)

def diag_ssm_scan(log_a, abar, bu, s0):
    bu_r, bu_i = bu
    if s0 is not None:
        s_r, s_i = s0
        bu_r = bu_r.at[:, 0].add(abar[0] * s_r - abar[1] * s_i)
        bu_i = bu_i.at[:, 0].add(abar[0] * s_i + abar[1] * s_r)
    counts = jnp.ones((1, bu_r.shape[1], 1, 1), jnp.float32)

    def combine(e1, e2):
        n1, r1, i1 = e1
        n2, r2, i2 = e2
        mag = jnp.exp(n2 * log_a[0])
        ang = n2 * log_a[1]
        pr, pi = mag * jnp.cos(ang), mag * jnp.sin(ang)
        return n1 + n2, pr * r1 - pi * i1 + r2, pr * i1 + pi * r1 + i2

    _, sr, si = lax.associative_scan(combine, (counts, bu_r, bu_i), axis=1)
    return sr, si

def s5_mixer(hc, hx, lam_re, lam_im, log_step, b_re, b_im, c_re, c_im, d_skip, w_glu):
    def groups(h):
        return h.astype(jnp.float32).reshape(h.shape[0], h.shape[1], S5_GROUPS, S5_GROUP)
    uc, ux = groups(hc), groups(hx)
    d_g = d_skip.astype(jnp.float32).reshape(S5_GROUPS, S5_GROUP)
    yc, yx = d_g * uc, d_g * ux
    for dn in range(2):
        log_a, abar, bbar = s5_discretise(lam_re[dn], lam_im[dn], log_step[dn], b_re, b_im)
        order = (lambda a: a) if dn == 0 else (lambda a: jnp.flip(a, axis=1))
        def drive(u):
            return (jnp.einsum('btgh,gph->btgp', u, bbar[0]), jnp.einsum('btgh,gph->btgp', u, bbar[1]))
        def read(s):
            return (jnp.einsum('btgp,ghp->btgh', s[0], c_re[dn].astype(jnp.float32))
                    - jnp.einsum('btgp,ghp->btgh', s[1], c_im[dn].astype(jnp.float32)))
        sc = diag_ssm_scan(log_a, abar, drive(order(uc)), None)
        sx = diag_ssm_scan(log_a, abar, drive(order(ux)), (sc[0][:, -1], sc[1][:, -1]))
        yc = yc + order(read(sc))
        yx = yx + order(read(sx))

    def glu(y, h):
        z = jax.nn.gelu(y.reshape(h.shape).astype(jnp.float32), approximate=False).astype(h.dtype)
        val, gate = jnp.split(z @ w_glu, 2, axis=-1)
        return val * jax.nn.sigmoid(gate)

    return glu(yc, hc), glu(yx, hx)

def peer_ffn(h, w_q, keys, u_tab, v_tab):
    bn, t, _ = h.shape
    q = (h @ w_q).astype(jnp.float32).reshape(bn, t, PEER_HEADS, 2, PEER_HALF)
    s = jnp.einsum('bthcd,hckd->bthck', q, keys.astype(jnp.float32))
    s_top, i_top = lax.top_k(s, PEER_TOPK)
    cand_s = (s_top[..., 0, :, None] + s_top[..., 1, None, :]).reshape(bn, t, PEER_HEADS, PEER_TOPK * PEER_TOPK)
    cand_i = (i_top[..., 0, :, None] * PEER_NKEYS + i_top[..., 1, None, :]).reshape(bn, t, PEER_HEADS, PEER_TOPK * PEER_TOPK)
    best_s, pos = lax.top_k(cand_s, PEER_TOPK)
    idx = jnp.take_along_axis(cand_i, pos, axis=-1)
    gates = jax.nn.softmax(best_s, axis=-1)
    n_blocks = bn * t // PEER_BLOCK
    n_sel = PEER_HEADS * PEER_TOPK
    hb = h.reshape(n_blocks, PEER_BLOCK, D_MODEL)
    ib = idx.reshape(n_blocks, PEER_BLOCK, n_sel)
    gb = gates.astype(h.dtype).reshape(n_blocks, PEER_BLOCK, n_sel)

    def experts(args):
        hh, ii, gg = args
        pre = jnp.einsum('ced,cd->ce', jnp.take(u_tab, ii, axis=0), hh)
        act = jax.nn.gelu(pre.astype(jnp.float32), approximate=False).astype(hh.dtype)
        return jnp.einsum('ce,ced->cd', act * gg, jnp.take(v_tab, ii, axis=0))

    return lax.map(experts, (hb, ib, gb)).reshape(bn, t, D_MODEL)

def setup_inputs(seed: int = 0) -> dict:
    key = jax.random.key(seed)
    ks = iter(jax.random.split(key, 40))
    nrm = lambda shape, scale: scale * jax.random.normal(next(ks), shape, jnp.float32)
    n_a, n_b, n_c = (_n_layers_of(kk) for kk in range(N_MIXERS))
    D = D_MODEL
    inv = D ** -0.5
    G, P, GC = S5_GROUPS, S5_STATE, S5_GROUP
    lam_im0 = math.pi * jnp.arange(P, dtype=jnp.float32)
    return {
        'x': nrm((BATCH, SEQ, D), 1.0),
        'c': nrm((BATCH, D), 1.0),
        'ctx': nrm((BATCH, CTX_LEN, D), 1.0),
        'c_ctx': nrm((D,), 1.0),
        'ada_w': nrm((DEPTH, D, 6 * D), 0.5 * inv),
        'ada_b': nrm((DEPTH, 6 * D), 0.02),
        'norm1_g': 1.0 + nrm((DEPTH, D), 0.02),
        'norm2_g': 1.0 + nrm((DEPTH, D), 0.02),
        'conv_w_in': nrm((n_a, D, 3 * D), inv),
        'conv_k': nrm((n_a, CONV_WIDTH, D), CONV_WIDTH ** -0.5),
        'conv_w_out': nrm((n_a, D, D), inv),
        'hgrn_w_in': nrm((n_b, D, 5 * D), inv),
        'hgrn_lb': nrm((DEPTH, 2, D), 0.1),
        'hgrn_norm_g': 1.0 + nrm((n_b, D), 0.02),
        'hgrn_w_out': nrm((n_b, D, D), inv),
        's5_lambda_re': -0.5 + nrm((n_c, 2, G, P), 0.01),
        's5_lambda_im': lam_im0 + nrm((n_c, 2, G, P), 0.01),
        's5_log_step': jax.random.uniform(next(ks), (n_c, 2, G), jnp.float32, math.log(S5_MIN_STEP), math.log(S5_MAX_STEP)),
        's5_b_re': nrm((n_c, G, P, GC), (2 * GC) ** -0.5),
        's5_b_im': nrm((n_c, G, P, GC), (2 * GC) ** -0.5),
        's5_c_re': nrm((n_c, 2, G, GC, P), (2 * P) ** -0.5),
        's5_c_im': nrm((n_c, 2, G, GC, P), (2 * P) ** -0.5),
        's5_d': nrm((n_c, D), 1.0),
        's5_w_glu': nrm((n_c, D, 2 * D), inv),
        'peer_w_q': nrm((DEPTH, D, PEER_HEADS * PEER_QDIM), inv),
        'peer_keys': nrm((DEPTH, PEER_HEADS, 2, PEER_NKEYS, PEER_HALF), PEER_HALF ** -0.5),
        'peer_u': nrm((DEPTH, PEER_EXPERTS, D), inv),
        'peer_v': nrm((DEPTH, PEER_EXPERTS, D), PEER_V_SCALE),
        'final_g': 1.0 + nrm((D,), 0.02),
    }

def reference(x, c, ctx, c_ctx, ada_w, ada_b, norm1_g, norm2_g, conv_w_in, conv_k, conv_w_out,
              hgrn_w_in, hgrn_lb, hgrn_norm_g, hgrn_w_out, s5_lambda_re, s5_lambda_im, s5_log_step,
              s5_b_re, s5_b_im, s5_c_re, s5_c_im, s5_d, s5_w_glu, peer_w_q, peer_keys, peer_u, peer_v,
              final_g):
    rows = x.shape[1] // GRID_W
    lb_soft = jax.nn.softmax(hgrn_lb.astype(jnp.float32), axis=0)
    lower_bounds = jnp.cumsum(lb_soft, axis=0) - lb_soft[0]
    xc = ctx
    for i in range(DEPTH):
        kind, j = i % N_MIXERS, i // N_MIXERS
        last = i == DEPTH - 1
        mx = [m[:, None, :] for m in adaln(c, ada_w[i], ada_b[i])]
        mc = adaln(c_ctx, ada_w[i], ada_b[i]) if (not last or kind != 0) else None
        hx = modulate(rms_norm(x, norm1_g[i]), mx[0], mx[1])
        if kind == 0:
            yx = short_conv_mixer(hx, conv_w_in[j], conv_k[j], conv_w_out[j], rows)
            yc = None if last else short_conv_mixer(modulate(rms_norm(xc, norm1_g[i]), mc[0], mc[1]),
                                                     conv_w_in[j], conv_k[j], conv_w_out[j], None)
        else:
            hc = modulate(rms_norm(xc, norm1_g[i]), mc[0], mc[1])
            if kind == 1:
                yc, yx = hgrn2_mixer(hc, hx, hgrn_w_in[j], lower_bounds[i], hgrn_norm_g[j], hgrn_w_out[j])
            else:
                yc, yx = s5_mixer(hc, hx, s5_lambda_re[j], s5_lambda_im[j], s5_log_step[j], s5_b_re[j],
                                  s5_b_im[j], s5_c_re[j], s5_c_im[j], s5_d[j], s5_w_glu[j])
        x = x + mx[2] * yx
        x = x + mx[5] * peer_ffn(modulate(rms_norm(x, norm2_g[i]), mx[3], mx[4]),
                                 peer_w_q[i], peer_keys[i], peer_u[i], peer_v[i])
        if not last:
            xc = xc + mc[2] * yc
            xc = xc + mc[5] * peer_ffn(modulate(rms_norm(xc, norm2_g[i]), mc[3], mc[4]),
                                       peer_w_q[i], peer_keys[i], peer_u[i], peer_v[i])
    return rms_norm(x, final_g)


_drawn_inputs = setup_inputs


def setup_inputs(seed=0):
    import zlib

    import numpy as np

    out = dict(_drawn_inputs(seed))
    spreads = {}
    factors = {'ctx': 8.0,
     'c_ctx': 8.0,
     'norm1_g': 2.881,
     'norm2_g': 26.456,
     'hgrn_lb': 8.0,
     'hgrn_norm_g': 42.514,
     'final_g': 2.717}
    for name, (base, spread) in spreads.items():
        noise = np.random.default_rng([zlib.crc32(name.encode()), seed]).standard_normal(out[name].shape)
        drawn = base * np.exp(spread * noise) if base else spread * noise
        out[name] = __import__('jax').numpy.asarray(drawn.astype(out[name].dtype))
    for name, factor in factors.items():
        out[name] = (out[name] * factor).astype(out[name].dtype)
    return out
```

```python
from contextlib import ExitStack

import concourse.bass as bass
from concourse import mybir
from concourse.alu_op_type import AluOpType as ALU

ACT = mybir.ActivationFunctionType
AX = mybir.AxisListType
F32 = mybir.dt.float32
F32R = mybir.dt.float32r
U32 = mybir.dt.uint32

P = 128
D = 1024
KC = D // P
SEQ, CTX = 512, 256
TOK = SEQ + CTX
GRID_W = 64
HEADS = 8
TOPK = 16
NKEYS = 128
LISTS = 2 * HEADS
CHUNK = 32
XCH = SEQ // CHUNK
CCH = CTX // CHUNK
NCH = XCH + CCH
EPS = 1e-6
LOWEST = -3.0e38
RAW = 4
SPLIT = 2
STAGE_T = 32
QUAD = 4
GROUPS = NKEYS // QUAD
AHEAD = 8


def halves(tokens):
    n = 1 if tokens <= 512 else 2
    return [(i * tokens // n, tokens // n) for i in range(n)]


class Trunk:

    def __init__(self, nc, ctx, a):
        self.nc, self.a = nc, a

        def sb(name, shape, dt=F32):
            return ctx.enter_context(nc.sbuf_tensor(name, shape, dt))

        def sem(name):
            return ctx.enter_context(nc.semaphore(name))

        self.own = []
        self.own_ctx = ExitStack()
        self.xT = sb("xT", [P, KC, TOK])
        self.h_hi = sb("h_hi", [P, KC, TOK], F32R)
        self.h_lo = sb("h_lo", [P, KC, TOK], F32R)
        self.raw = sb("w_raw", [P, RAW, D])
        self.w_hi = sb("w_hi", [P, SPLIT, D], F32R)
        self.w_lo = sb("w_lo", [P, SPLIT, D], F32R)
        self.ident = sb("ident", [P, P])
        self.ones = sb("ones", [P, P])
        self.iota = sb("iota", [P, P])
        self.eps = sb("eps", [P, 1])
        self.mod = sb("mod", [P, 2, 2, 48])
        self.gs = sb("gs", [P, 2, 2, 2, KC])
        self.gains = sb("gains", [P, 6, KC])
        self.lb = sb("lb", [P, 2, 2, KC])
        self.psum = ctx.enter_context(nc.psum_tensor("psum", [P, 8, 512], F32))
        self.raw_in = [sem(f"raw_in{i}") for i in range(RAW)]
        self.raw_at = [0] * RAW
        self.hi_done = sem("w_hi_done")
        self.lo_done = sem("w_lo_done")
        self.tile_done = sem("tile_product_done")
        self.acc_free = [sem(f"acc_free{x}") for x in range(2)]
        self.settled = sem("settled")
        self.tiles = 0

    def sem(self, name):
        self.own.append(self.own_ctx.enter_context(self.nc.semaphore(name)))
        return self.own[-1]

    def retire(self):
        with self.nc.Block() as block:

            @block.gpsimd
            def _(pool):
                for s in self.own:
                    pool.sem_clear(s)
        self.own = []
        self.own_ctx.close()

    def settle(self, eng):
        eng.sem_inc(self.settled, 1)

    def load(self, sp, src, i, slot, n_raw, turn):
        sp.wait_ge(self.lo_done, i + (self.tiles + RAW - n_raw + 1))
        sp.dma_start(self.raw[:, slot, :], src).then_inc(self.raw_in[slot], 16)

    def hi(self, act, i, slot, s, turn):
        act.wait_ge(self.raw_in[slot], turn * 16 + (self.raw_at[slot] + 16))
        act.wait_ge(self.tile_done, i + (self.tiles + 1))
        act.activation(self.w_hi[:, s, :], self.raw[:, slot, :], ACT.Copy).then_inc(self.hi_done, 1)

    def lo(self, pool, i, slot, s):
        pool.wait_ge(self.hi_done, i + (self.tiles + 1))
        pool.tensor_tensor(self.w_lo[:, s, :], self.raw[:, slot, :], self.w_hi[:, s, :].bitcast(F32),
                           ALU.subtract).then_inc(self.lo_done, 1)

    def product(self, pe, i, s, tokens, hi, lo, ks=range(KC)):
        if ks[0] == 0:
            pe.wait_ge(self.lo_done, i + (self.tiles + RAW + 1))
            pe.wait_ge(self.acc_free[s], i // 2 + (self.tiles // 2 + 1))
        for k in ks:
            wh = self.w_hi[:, s, k * P:(k + 1) * P]
            wl = self.w_lo[:, s, k * P:(k + 1) * P]
            for n, (t0, w) in enumerate(halves(tokens)):
                out = self.psum[:, 2 * s + n, 0:w]
                pe.matmul(out, wh, hi[:, k, t0:t0 + w], start=(k == 0), stop=False)
                pe.matmul(out, wh, lo[:, k, t0:t0 + w], start=False, stop=False)
                last = pe.matmul(out, wl, hi[:, k, t0:t0 + w], start=False, stop=(k == KC - 1))
        if ks[-1] == KC - 1:
            last.then_inc(self.tile_done, 1)

    def wait_product(self, eng, i):
        eng.wait_ge(self.tile_done, i + (self.tiles + SPLIT + 1))

    def acc(self, s, tokens):
        hv = halves(tokens)
        return self.psum[:, 2 * s:2 * s + len(hv), 0:hv[0][1]]

    def end_stage(self, n, n_raw):
        self.tiles += n
        for s in range(n_raw):
            self.raw_at[s] += 16 * n // n_raw


def split_tokens(ap, tokens):
    return ap.rearrange("p (h w) -> p h w", h=len(halves(tokens)))


def stage_setup(t):
    nc, a = t.nc, t.a
    with ExitStack() as ctx:
        sb = lambda n, s, d=F32: ctx.enter_context(nc.sbuf_tensor(n, s, d))
        cond = sb("cond", [P, KC, 2])
        scond = sb("scond", [P, KC, 2])
        bias = sb("ada_bias", [P, 2, 48])
        lbr = sb("lb_raw", [P, 2, 2, KC])
        lbm = sb("lb_max", [P, 2, KC])
        lbe = sb("lb_exp", [P, 2, 2, KC])
        lbs = sb("lb_sum", [P, 2, KC])
        row = sb("mod_row", [2, 2, 6 * D])
        aw = sb("ada_w", [P, 3, KC, 512])
        small_in, x_in = t.sem("small_in"), t.sem("x_in")
        aw_in = [t.sem(f"ada_in{i}") for i in range(3)]
        const_done, id_zero = t.sem("const_done"), t.sem("id_zero")
        silu_done, row_mm, row_out = t.sem("silu_done"), t.sem("row_mm"), t.sem("row_out")
        flipped, mod_done, lb_step, lb_exp = t.sem("flipped"), t.sem("mod_done"), t.sem("lb_step"), t.sem("lb_exp")
        N = 6 * D // 512
        with nc.Block() as block:

            @block.sync
            def _(sp):
                sp.dma_start(cond[:], a["cond"]).then_inc(small_in, 16)
                sp.dma_start(t.gains[:], a["gains"]).then_inc(small_in, 16)
                sp.dma_start(bias[:], a["ada_b"]).then_inc(small_in, 16)
                sp.dma_start(lbr[:], a["hgrn_lb"]).then_inc(small_in, 16)
                with sp.Fori(0, 2 * N // 3) as q:
                    for s in range(3):
                        sp.wait_ge(row_mm, q * 3 + (s + 1))
                        sp.dma_start(aw[:, s], a["ada_w"][bass.ds(q * 3 + s, 1)].rearrange(
                            "a p k n -> p (a k) n")).then_inc(aw_in[s], 16)
                sp.dma_start(t.xT[:, :, 0:SEQ], a["x"]).then_inc(x_in, 16)
                sp.dma_start(t.xT[:, :, SEQ:TOK], a["ctx"]).then_inc(x_in, 16)
                sp.wait_ge(x_in, 32)

            @block.gpsimd
            def _(pool):
                pool.memset(t.ident[:], 0.0).then_inc(id_zero, 1)
                pool.memset(t.ones[:], 1.0).then_inc(const_done, 1)
                pool.memset(t.eps[:], EPS).then_inc(const_done, 1)
                pool.iota(t.iota[:], pattern=[[1, P]], base=0, channel_multiplier=0,
                          allow_small_or_imprecise_dtypes=True).then_inc(const_done, 1)
                pool.wait_ge(id_zero, 1)
                pool.affine_select(out=t.ident[:], in_=t.ident[:], compare_op=ALU.not_equal, fill=1.0,
                                   base=0, pattern=[[-1, P]], channel_multiplier=1).then_inc(const_done, 1)
                pool.wait_ge(const_done, 4)

            @block.scalar
            def _(act):
                act.wait_ge(small_in, 64)
                act.activation(scond[:], cond[:], ACT.Silu).then_inc(silu_done, 1)
                act.wait_ge(lb_step, 2)
                act.activation(lbe[:], lbr[:], ACT.Exp).then_inc(lb_exp, 1)
                with act.Fori(0, N) as q:
                    for s in range(2):
                        act.wait_ge(row_mm, q * 2 + (3 + s + 1))
                        act.activation(row[:, :, :].rearrange("c l n -> c (l n)")[
                            :, bass.ds(q * 1024 + s * 512, 512)], t.psum[0:2, s, :], ACT.Copy
                        ).then_inc(row_out, 1)

            @block.tensor
            def _(pe):
                pe.sem_inc(row_mm, 3)
                pe.sem_inc(row_out, 2)
                pe.sem_inc(t.lo_done, RAW)
                pe.sem_inc(t.tile_done, SPLIT)
                for x in range(2):
                    pe.sem_inc(t.acc_free[x], 1)
                pe.wait_ge(silu_done, 1)
                with pe.Fori(0, 2 * N // 6) as q:
                    for i in range(6):
                        pe.wait_ge(aw_in[i % 3], q * 32 + 16 * (i // 3 + 1))
                        pe.wait_ge(row_out, q * 6 + (i + 1))
                        for k in range(KC):
                            last = pe.matmul(t.psum[0:2, i % 2, :], scond[:, k, :], aw[:, i % 3, k, :],
                                             start=(k == 0), stop=(k == KC - 1))
                        last.then_inc(row_mm, 1)
                pe.wait_ge(row_out, 2 * N + 2)
                pe.wait_ge(const_done, 4)
                for layer in range(2):
                    for j in range(48):
                        last = pe.transpose(t.psum[:, 2 + layer, 2 * j:2 * j + 2],
                                            row[:, layer, j * P:(j + 1) * P], t.ident[0:2, 0:2])
                    last.then_inc(flipped, 1)

            @block.vector
            def _(dve):
                dve.wait_ge(small_in, 64)
                dve.tensor_tensor(lbm[:], lbr[:, 0], lbr[:, 1], ALU.max).then_inc(lb_step, 1)
                dve.wait_ge(lb_step, 1)
                dve.tensor_tensor(lbr[:], lbr[:], lbm[:].unsqueeze(1).to_broadcast([P, 2, 2, KC]),
                                  ALU.subtract).then_inc(lb_step, 1)
                dve.wait_ge(lb_exp, 1)
                dve.tensor_tensor(lbs[:], lbe[:, 0], lbe[:, 1], ALU.add).then_inc(lb_step, 1)
                dve.wait_ge(lb_step, 3)
                dve.reciprocal(lbm[:], lbs[:]).then_inc(lb_step, 1)
                dve.wait_ge(lb_step, 4)
                dve.tensor_tensor(lbr[:], lbe[:], lbm[:].unsqueeze(1).to_broadcast([P, 2, 2, KC]),
                                  ALU.mult).then_inc(lb_step, 1)
                dve.wait_ge(lb_step, 5)
                dve.tensor_tensor(lbs[:], lbr[:, 0], lbr[:, 1], ALU.add).then_inc(lb_step, 1)
                dve.wait_ge(lb_step, 6)
                dve.tensor_tensor(t.lb[:, 0], lbs[:], lbr[:, 0], ALU.subtract).then_inc(lb_step, 1)
                dve.wait_ge(lb_step, 7)
                dve.tensor_scalar(t.lb[:, 1], t.lb[:, 0], -1.0, 1.0, ALU.mult, ALU.add).then_inc(lb_step, 1)
                for layer in range(2):
                    dve.wait_ge(flipped, layer + 1)
                    dve.tensor_tensor(t.mod[:, layer], t.psum[:, 2 + layer, 0:96].rearrange(
                        "p (j c) -> p c j", c=2), bias[:, layer].unsqueeze(1).to_broadcast([P, 2, 48]),
                        ALU.add).then_inc(mod_done, 1)
                dve.wait_ge(mod_done, 2)
                for layer in range(2):
                    for n in range(2):
                        at = 24 * n + KC
                        dve.scalar_tensor_tensor(
                            out=t.gs[:, layer, n], in0=t.mod[:, layer, :, at:at + KC], scalar=1.0,
                            in1=t.gains[:, 2 * n + layer].unsqueeze(1).to_broadcast([P, 2, KC]),
                            op0=ALU.add, op1=ALU.mult).then_inc(mod_done, 1)
                dve.wait_ge(mod_done, 6)
                dve.wait_ge(lb_step, 8)


def stage_norm(t, layer, n, tokens):
    nc = t.nc
    final = n == 2
    tag = f"n{layer}{n}"
    hv = halves(tokens)
    segs = [(0, SEQ, 0)] + ([(SEQ, CTX, 1)] if tokens == TOK else [])
    with ExitStack() as ctx:
        sb = lambda nm, s, d=F32: ctx.enter_context(nc.sbuf_tensor(nm + tag, s, d))
        sq = sb("sq", [P, 2, tokens])
        rs = sb("rs", [P, tokens])
        rstd = sb("rstd", [P, tokens])
        xn = sb("xn", [P, 2, tokens])
        hf = sb("hf", [P, 2, tokens])
        out = sb("out", [P, KC, tokens]) if final else None
        sq_done, sum_part, root, rstd_done = (t.sem(s + tag) for s in ("sq", "sums", "root", "rstd"))
        xn_done, hf_done, hi_done, lo_done = (t.sem(s + tag) for s in ("xn_", "hf_", "hi_", "lo_"))
        stored = t.sem("stored" + tag) if final else None
        with nc.Block() as block:

            @block.scalar
            def _(act):
                for k in range(KC):
                    if k >= 2:
                        act.wait_ge(sum_part, k - 1)
                    act.activation(sq[:, k % 2], t.xT[:, k, 0:tokens], ACT.Square).then_inc(sq_done, 1)
                act.wait_ge(sum_part, KC)
                act.activation(split_tokens(rs[:], tokens), t.acc(0, tokens), ACT.Sqrt, bias=t.eps[:],
                               scale=1.0 / D).then_inc(root, 1)
                if final:
                    return
                for k in range(KC):
                    act.wait_ge(xn_done, k + 1)
                    if k >= 2:
                        act.wait_ge(lo_done, k - 1)
                    for t0, w, c in segs:
                        at = 24 * n + k
                        last = act.activation(hf[:, k % 2, t0:t0 + w], xn[:, k % 2, t0:t0 + w], ACT.Identity,
                                              bias=t.mod[:, layer, c, at:at + 1],
                                              scale=t.gs[:, layer, n, c, k:k + 1])
                        last.then_inc(hf_done, 1)
                    act.wait_ge(hf_done, len(segs) * (k + 1))
                    act.activation(t.h_hi[:, k, 0:tokens], hf[:, k % 2], ACT.Copy).then_inc(hi_done, 1)

            @block.tensor
            def _(pe):
                for k in range(KC):
                    pe.wait_ge(sq_done, k + 1)
                    for i, (t0, w) in enumerate(hv):
                        last = pe.matmul(t.psum[:, i, 0:w], t.ones[:], sq[:, k % 2, t0:t0 + w],
                                         start=(k == 0), stop=(k == KC - 1))
                    last.then_inc(sum_part, 1)

            @block.vector
            def _(dve):
                dve.wait_ge(root, 1)
                dve.reciprocal(rstd[:], rs[:]).then_inc(rstd_done, 1)
                dve.wait_ge(rstd_done, 1)
                for k in range(KC):
                    if final:
                        dve.scalar_tensor_tensor(out=out[:, k], in0=t.xT[:, k, 0:tokens],
                                                 scalar=t.gains[:, 4, k:k + 1], in1=rstd[:], op0=ALU.mult,
                                                 op1=ALU.mult).then_inc(xn_done, 1)
                        continue
                    if k >= 2:
                        dve.wait_ge(hf_done, len(segs) * (k - 1))
                    dve.tensor_tensor(xn[:, k % 2], t.xT[:, k, 0:tokens], rstd[:], ALU.mult).then_inc(xn_done, 1)
                    dve.wait_ge(hi_done, k + 1)
                    dve.tensor_tensor(t.h_lo[:, k, 0:tokens], hf[:, k % 2],
                                      t.h_hi[:, k, 0:tokens].bitcast(F32), ALU.subtract).then_inc(lo_done, 1)
                if not final:
                    dve.wait_ge(lo_done, KC)

            @block.sync
            def _(sp):
                if final:
                    for k in range(KC):
                        sp.wait_ge(xn_done, k + 1)
                        sp.dma_start(t.a["out"][:, k], out[:, k]).then_inc(stored, 16)
                    sp.wait_ge(stored, 16 * KC)


def conv_rows():
    return [(0, SEQ // GRID_W, GRID_W), (SEQ, 1, CTX)]


def stage_conv(t, y_hi, y_lo):
    nc = t.nc
    T = TOK
    n = 3 * KC
    BODY = 12
    with ExitStack() as ctx:
        sb = lambda nm, s, d=F32: ctx.enter_context(nc.sbuf_tensor(nm, s, d))
        kern = sb("kern", [P, KC, 3])
        gc = sb("gate_c", [P, T])
        z = sb("z", [P, T])
        zc = sb("zc", [P, T])
        y = sb("y", [P, T])
        k_in = t.sem("kern_in")
        gc_done, z_done, conv_step = t.sem("gc_done"), t.sem("z_done"), t.sem("conv_step")
        y_done, yhi_done, ylo_done = t.sem("y_done"), t.sem("yhi_done"), t.sem("ylo_done")
        STEPS = 5
        with nc.Block() as block:

            @block.sync
            def _(sp):
                sp.dma_start(kern[:], t.a["conv_k"]).then_inc(k_in, 16)
                with sp.Fori(0, n // BODY) as q:
                    for i in range(BODY):
                        t.load(sp, t.a["conv_w_in"][bass.ds(q * BODY + i, 1)].rearrange("a p n -> p (a n)"),
                               q * BODY + i, i % RAW, RAW, None)

            @block.gpsimd
            def _(pool):
                with pool.Fori(0, n // BODY) as q:
                    for i in range(BODY):
                        t.lo(pool, q * BODY + i, i % RAW, i % SPLIT)

            @block.tensor
            def _(pe):
                with pe.Fori(0, n // BODY) as q:
                    for i in range(BODY):
                        t.product(pe, q * BODY + i, i % SPLIT, T, t.h_hi, t.h_lo)

            @block.scalar
            def _(act):
                def evac(q, i):
                    m = i // 3
                    c = q * (BODY // 3) + m
                    if i % 3 == 0:
                        t.wait_product(act, q * BODY + i)
                        act.wait_ge(z_done, c + 1)
                        act.activation(split_tokens(gc[:], T), t.acc(i % SPLIT, T), ACT.Copy).then_inc(gc_done, 1)
                        act.wait_ge(gc_done, c + 1)
                        act.sem_inc(t.acc_free[i % SPLIT], 1)
                    if i % 3 == 2:
                        act.wait_ge(y_done, c + 1)
                        act.activation(y_hi[:, bass.ds(c, 1), :].rearrange("p a n -> p (a n)"), y[:],
                                       ACT.Copy).then_inc(yhi_done, 1)
                with act.Fori(0, n // BODY) as q:
                    for i in range(BODY):
                        t.hi(act, q * BODY + i, i % RAW, i % SPLIT, q * (BODY // RAW) + i // RAW)
                        if i >= 1:
                            evac(q, i - 1)
                    evac(q, BODY - 1)

            @block.vector
            def _(dve):
                dve.sem_inc(z_done, 1)
                dve.sem_inc(ylo_done, 1)
                dve.wait_ge(k_in, 16)
                with dve.Fori(0, n // BODY) as q:
                    for m in range(BODY // 3):
                        c = q * (BODY // 3) + m
                        i = 3 * m
                        t.wait_product(dve, q * BODY + (i + 1))
                        dve.wait_ge(gc_done, c + 1)
                        dve.tensor_tensor(split_tokens(z[:], T), split_tokens(gc[:], T),
                                          t.acc((i + 1) % SPLIT, T), ALU.mult).then_inc(z_done, 1)
                        dve.wait_ge(z_done, c + 2)
                        dve.sem_inc(t.acc_free[(i + 1) % SPLIT], 1)
                        kk = kern[:, bass.ds(c, 1), :].rearrange("p a n -> p (a n)")
                        dve.tensor_scalar(zc[:], z[:], kk[:, 1:2], None, ALU.mult).then_inc(conv_step, 1)
                        s = 1
                        for tap in (0, 2):
                            dve.wait_ge(conv_step, c * STEPS + s)
                            for t0, rows, w in conv_rows():
                                zr = z[:, t0:t0 + rows * w].rearrange("p (r w) -> p r w", w=w)
                                cr = zc[:, t0:t0 + rows * w].rearrange("p (r w) -> p r w", w=w)
                                src = zr[:, :, 0:w - 1] if tap == 0 else zr[:, :, 1:w]
                                dst = cr[:, :, 1:w] if tap == 0 else cr[:, :, 0:w - 1]
                                dve.scalar_tensor_tensor(out=dst, in0=src, scalar=kk[:, tap:tap + 1], in1=dst,
                                                         op0=ALU.mult, op1=ALU.add).then_inc(conv_step, 1)
                                s += 1
                        t.wait_product(dve, q * BODY + (i + 2))
                        dve.wait_ge(conv_step, c * STEPS + STEPS)
                        dve.wait_ge(ylo_done, c + 1)
                        dve.tensor_tensor(split_tokens(y[:], T), split_tokens(zc[:], T),
                                          t.acc((i + 2) % SPLIT, T), ALU.mult).then_inc(y_done, 1)
                        dve.wait_ge(y_done, c + 1)
                        dve.sem_inc(t.acc_free[(i + 2) % SPLIT], 1)
                        dve.wait_ge(yhi_done, c + 1)
                        dve.tensor_tensor(y_lo[:, bass.ds(c, 1), :].rearrange("p a n -> p (a n)"), y[:],
                                          y_hi[:, bass.ds(c, 1), :].rearrange("p a n -> p (a n)").bitcast(F32),
                                          ALU.subtract).then_inc(ylo_done, 1)
                dve.wait_ge(ylo_done, KC + 1)
        t.end_stage(n, RAW)


def stage_mix_out(t, layer, w_name, tokens, y_hi, y_lo):
    nc = t.nc
    segs = [(0, SEQ, 0)] + ([(SEQ, CTX, 1)] if tokens == TOK else [])
    with ExitStack() as ctx:
        tmp = ctx.enter_context(nc.sbuf_tensor(f"mix{layer}", [P, 2, tokens], F32))
        copied, added = t.sem(f"mix_copied{layer}"), t.sem(f"mix_added{layer}")
        with nc.Block() as block:

            @block.sync
            def _(sp):
                for i in range(KC):
                    t.load(sp, t.a[w_name][i], i, i % RAW, RAW, None)

            @block.gpsimd
            def _(pool):
                for i in range(KC):
                    t.lo(pool, i, i % RAW, i % SPLIT)

            @block.tensor
            def _(pe):
                for i in range(KC):
                    t.product(pe, i, i % SPLIT, tokens, y_hi, y_lo)

            @block.scalar
            def _(act):
                def evac(i):
                    t.wait_product(act, i)
                    if i >= 2:
                        act.wait_ge(added, len(segs) * (i - 1))
                    act.activation(split_tokens(tmp[:, i % 2], tokens), t.acc(i % SPLIT, tokens),
                                   ACT.Copy).then_inc(copied, 1)
                    act.wait_ge(copied, i + 1)
                    act.sem_inc(t.acc_free[i % SPLIT], 1)
                for i in range(KC):
                    t.hi(act, i, i % RAW, i % SPLIT, i // RAW)
                    if i >= 1:
                        evac(i - 1)
                evac(KC - 1)

            @block.vector
            def _(dve):
                for i in range(KC):
                    dve.wait_ge(copied, i + 1)
                    for t0, w, c in segs:
                        dve.scalar_tensor_tensor(out=t.xT[:, i, t0:t0 + w], in0=tmp[:, i % 2, t0:t0 + w],
                                                 scalar=t.mod[:, layer, c, 16 + i:17 + i],
                                                 in1=t.xT[:, i, t0:t0 + w], op0=ALU.mult,
                                                 op1=ALU.add).then_inc(added, 1)
                dve.wait_ge(added, len(segs) * KC)
        t.end_stage(KC, RAW)


def stage_rank(t, layer, tokens, top, top_i):
    nc = t.nc
    blocks = tokens // P
    n, BODY = LISTS, 4
    tag = f"r{layer}"
    with ExitStack() as ctx:
        sb = lambda nm, s, d=F32: ctx.enter_context(nc.sbuf_tensor(nm + tag, s, d))
        keys = sb("keys", [P, LISTS, NKEYS])
        qT = sb("qT", [P, 2, tokens])
        sc = sb("sc", [P, 2, blocks, NKEYS])
        t8 = sb("t8", [P, 2, blocks, 2, 8])
        i8 = sb("i8", [P, 2, blocks, 2, 8], U32)
        k_in, q_done, s_mm, s_done = (t.sem(x + tag) for x in ("keys_in", "q_done", "s_mm", "s_done"))
        rank, taken, taken_v, s_cp = (t.sem(x + tag) for x in ("rank", "taken", "taken_v", "s_cp"))

        def score_bank(b):
            return t.psum[:, 4 + b // 4, (b % 4) * P:(b % 4 + 1) * P]

        with nc.Block() as block:

            @block.sync
            def _(sp):
                sp.dma_start(keys[:], t.a["peer_keys"][layer]).then_inc(k_in, 16)
                with sp.Fori(0, n // BODY) as q:
                    for i in range(BODY):
                        t.load(sp, t.a[f"peer_w_q{layer}"][bass.ds(q * BODY + i, 1)].rearrange(
                            "a p n -> p (a n)"), q * BODY + i, i % RAW, RAW, None)

            @block.gpsimd
            def _(pool):
                with pool.Fori(0, n // BODY) as q:
                    for i in range(BODY):
                        t.lo(pool, q * BODY + i, i % RAW, i % SPLIT)

            @block.tensor
            def _(pe):
                pe.wait_ge(k_in, 16)

                def scores(c, i):
                    pe.wait_ge(q_done, c + 1)
                    pe.wait_ge(s_done, c + 1)
                    for b in range(blocks):
                        last = pe.matmul(score_bank(b), qT[:, i % 2, b * P:(b + 1) * P],
                                         keys[:, bass.ds(c, 1), :].rearrange("p a n -> p (a n)"),
                                         start=True, stop=True)
                    last.then_inc(s_mm, 1)
                t.product(pe, 0, 0, tokens, t.h_hi, t.h_lo)
                with pe.Fori(0, n // BODY - 1) as q:
                    for i in range(BODY):
                        t.product(pe, q * BODY + (i + 1), (i + 1) % SPLIT, tokens, t.h_hi, t.h_lo)
                        scores(q * BODY + i, i)
                for i in range(n - BODY, n):
                    if i + 1 < n:
                        t.product(pe, i + 1, (i + 1) % SPLIT, tokens, t.h_hi, t.h_lo)
                    scores(i, i)

            @block.scalar
            def _(act):
                act.sem_inc(s_done, 1)
                act.sem_inc(taken, 2)

                def query(c, i):
                    t.wait_product(act, c)
                    act.wait_ge(s_mm, c + 1)
                    act.activation(split_tokens(qT[:, i % 2], tokens), t.acc(i % SPLIT, tokens),
                                   ACT.Copy).then_inc(q_done, 1)
                    act.wait_ge(q_done, c + 1)
                    act.sem_inc(t.acc_free[i % SPLIT], 1)

                def score(c, i):
                    act.wait_ge(s_mm, c + 3)
                    act.wait_ge(taken, c + 1)
                    for h in range(0, blocks, 4):
                        m = min(4, blocks - h)
                        last = act.activation(sc[:, i % 2, h:h + m], t.psum[:, 4 + h // 4, 0:m * P].rearrange(
                            "p (b k) -> p b k", k=P), ACT.Copy)
                        last.then_inc(s_cp, 1)
                    act.wait_ge(s_cp, (c + 1) * ((blocks + 3) // 4))
                    act.sem_inc(s_done, 1)
                act.sem_inc(s_mm, 2)
                for i in range(SPLIT):
                    t.hi(act, i, i % RAW, i % SPLIT, 0)
                with act.Fori(0, n // BODY - 1) as q:
                    for i in range(BODY):
                        c = q * BODY + i
                        query(c, i)
                        t.hi(act, c + SPLIT, (i + SPLIT) % RAW, i % SPLIT, q + (i + SPLIT) // RAW)
                        score(c, i)
                for i in range(n - BODY, n):
                    query(i, i)
                    if i + SPLIT < n:
                        t.hi(act, i + SPLIT, (i + SPLIT) % RAW, i % SPLIT, (i + SPLIT) // RAW)
                    score(i, i)

            @block.vector
            def _(dve):
                with dve.Fori(0, n // BODY) as q:
                    for i in range(BODY):
                        c = q * BODY + i
                        s = i % 2
                        dve.wait_ge(s_done, c + 2)
                        t.settle(dve)
                        for b in range(blocks):
                            dve.max(t8[:, s, b, 0], sc[:, s, b]).then_inc(rank, 1)
                        dve.wait_ge(rank, c * (5 * blocks) + blocks)
                        t.settle(dve)
                        for b in range(blocks):
                            dve.max_index(i8[:, s, b, 0], t8[:, s, b, 0], sc[:, s, b]).then_inc(rank, 1)
                        dve.wait_ge(rank, c * (5 * blocks) + 2 * blocks)
                        t.settle(dve)
                        for b in range(blocks):
                            dve.match_replace(sc[:, s, b], t8[:, s, b, 0], sc[:, s, b], LOWEST).then_inc(rank, 1)
                        dve.wait_ge(rank, c * (5 * blocks) + 3 * blocks)
                        t.settle(dve)
                        for b in range(blocks):
                            dve.max(t8[:, s, b, 1], sc[:, s, b]).then_inc(rank, 1)
                        dve.wait_ge(rank, c * (5 * blocks) + 4 * blocks)
                        t.settle(dve)
                        for b in range(blocks):
                            dve.max_index(i8[:, s, b, 1], t8[:, s, b, 1], sc[:, s, b]).then_inc(rank, 1)
                        dve.wait_ge(rank, c * (5 * blocks) + 5 * blocks)
                        dst = lambda x: x[:, :, bass.ds(c, 1), :].rearrange("p b a k -> p b (a k)")
                        dve.tensor_copy(dst(top), t8[:, s].rearrange("p b a k -> p b (a k)")).then_inc(taken_v, 1)
                        dve.tensor_copy(dst(top_i), i8[:, s].rearrange("p b a k -> p b (a k)")).then_inc(taken_v, 1)
                        dve.wait_ge(taken_v, c * 2 + 2)
                        dve.sem_inc(taken, 1)
        t.end_stage(n, RAW)


def stage_gates(t, layer, tokens, top, top_i, g_dram, act_dram):
    nc = t.nc
    PRE = AHEAD // 2
    blocks = tokens // P
    tag = f"g{layer}"
    K = TOPK
    STAGES, STEPS_S = P // STAGE_T, STAGE_T // 8
    with ExitStack() as ctx:
        sb = lambda nm, s, d=F32: ctx.enter_context(nc.sbuf_tensor(nm + tag, s, d))
        cand = sb("cand", [P, HEADS, K, K])
        pick = sb("pick", [P, HEADS, K, K])
        best = sb("best", [P, HEADS, K])
        pos = sb("pos", [P, HEADS, K], U32)
        half_u = sb("half_u", [P, 2, HEADS * K], U32)
        half = sb("half", [P, 2, HEADS * K])
        topf = sb("topf", [P, LISTS, K])
        sel = sb("sel", [P, 3, HEADS * K])
        ex = sb("ex", [P, HEADS, K])
        den = sb("den", [P, HEADS])
        selT = sb("selT", [P, 3, P])
        oi = sb("oi", [P, 8, P])
        oj = sb("oj", [P, 8, P])
        stage = sb("stage", [P, 2, NKEYS, STAGE_T])
        act_f = sb("act_g", [P, 2, tokens])
        gelu_done = t.sem("gelu_done" + tag)
        spilled = [t.sem(f"spilled{x}{tag}") for x in range(2)]
        dv, ex_in, ex_done = (t.sem(x + tag) for x in ("dv", "ex_in", "ex_done"))
        sel_T, selT_cp, oh_ready, g_mm, g_cp = (t.sem(x + tag) for x in ("sel_T", "selT_cp", "oh_ready", "g_mm", "g_cp"))
        stored = [t.sem(f"stored{x}{tag}") for x in range(2)]
        DV = 1 + 5 + 2 + 1 + 2 * 3 + 3 + 1
        with nc.Block() as block:

            @block.vector
            def _(dve):
                dve.sem_inc(g_mm, 2)
                dve.sem_inc(selT_cp, 1)
                bc = lambda ap, shape: ap.to_broadcast(shape)
                with dve.Fori(0, blocks) as b:
                    n = [0]

                    def step(ins):
                        n[0] += 1
                        ins.then_inc(dv, 1)
                        dve.wait_ge(dv, b * DV + n[0])
                    tb = top[:, bass.ds(b, 1), :, :].rearrange("p a (h c) k -> p (a h) c k", c=2)
                    step(dve.tensor_tensor(cand[:], bc(tb[:, :, 0, :].unsqueeze(3), [P, HEADS, K, K]),
                                           bc(tb[:, :, 1, :].unsqueeze(2), [P, HEADS, K, K]), ALU.add))
                    flat = lambda h: cand[:, h].rearrange("p a b -> p (a b)")
                    for part in range(2):
                        o = 8 * part
                        t.settle(dve)
                        for h in range(HEADS):
                            last = dve.max(best[:, h, o:o + 8], flat(h))
                        step(last)
                        t.settle(dve)
                        for h in range(HEADS):
                            last = dve.max_index(pos[:, h, o:o + 8], best[:, h, o:o + 8], flat(h))
                        step(last)
                        if part == 0:
                            t.settle(dve)
                            for h in range(HEADS):
                                last = dve.match_replace(flat(h), best[:, h, 0:8], flat(h), LOWEST)
                            step(last)
                    pf = pos[:].rearrange("p h k -> p (h k)")
                    dve.tensor_single_scalar(half_u[:, 0], pf, 4, ALU.logical_shift_right)
                    step(dve.tensor_single_scalar(half_u[:, 1], pf, 15, ALU.bitwise_and))
                    dve.tensor_copy(topf[:], top_i[:, bass.ds(b, 1), :, :].rearrange("p a l k -> p (a l) k"))
                    step(dve.tensor_copy(half[:], half_u[:]))
                    step(dve.tensor_tensor(ex[:], best[:], bc(best[:, :, 0:1], [P, HEADS, K]), ALU.subtract))
                    dve.sem_inc(ex_in, 1)
                    tf = topf[:].rearrange("p (h c) k -> p h c k", c=2)
                    for c in range(2):
                        step(dve.tensor_tensor(
                            pick[:], bc(half[:, c].rearrange("p (h k) -> p h k", k=K).unsqueeze(3), [P, HEADS, K, K]),
                            bc(t.iota[:, 0:K].unsqueeze(1).unsqueeze(1), [P, HEADS, K, K]), ALU.is_equal))
                        step(dve.tensor_tensor(pick[:], pick[:], bc(tf[:, :, c, :].unsqueeze(2), [P, HEADS, K, K]),
                                               ALU.mult))
                        step(dve.tensor_reduce(sel[:, c].rearrange("p (h k) -> p h k", k=K), pick[:], AX.X, ALU.add))
                    dve.wait_ge(ex_done, b + 1)
                    step(dve.tensor_reduce(den[:], ex[:], AX.X, ALU.add))
                    step(dve.reciprocal(den[:], den[:]))
                    step(dve.tensor_tensor(sel[:, 2].rearrange("p (h k) -> p h k", k=K), ex[:],
                                           bc(den[:].unsqueeze(2), [P, HEADS, K]), ALU.mult))
                    dve.wait_ge(sel_T, b + 1)
                    dve.wait_ge(g_mm, b * (P // 4) + 2)
                    step(dve.tensor_copy(selT[:], t.psum[:, 6, 0:3 * P].rearrange("p (c x) -> p c x", x=P)))
                    dve.sem_inc(selT_cp, 1)
                    for q in range(P // 8):
                        for u in range(2):
                            dve.wait_ge(g_mm, b * (P // 4) + q * 2 + (u + 1))
                            for r in range(4 * u, 4 * u + 4):
                                col = lambda c: selT[:, c, q * 8 + r:q * 8 + r + 1]
                                dve.tensor_scalar(oi[:, r], t.iota[:], col(0), None, ALU.is_equal)
                                last = dve.tensor_scalar(oj[:, r], t.iota[:], col(1), col(2), ALU.is_equal, ALU.mult)
                            last.then_inc(oh_ready, 1)
                assert n[0] == DV, n

            @block.tensor
            def _(pe):
                pe.sem_inc(g_cp, 2)
                up = lambda c, i, ks=range(KC): t.product(pe, c, i % SPLIT, tokens, t.h_hi, t.h_lo, ks)
                with pe.Fori(0, blocks) as b:
                    for i in range(PRE):
                        up(b * AHEAD + i, i)
                    pe.wait_ge(dv, b * DV + (DV - 1))
                    pe.wait_ge(selT_cp, b + 1)
                    for c in range(3):
                        last = pe.transpose(t.psum[:, 6, c * P:(c + 1) * P], sel[:, c], t.ident[:])
                    last.then_inc(sel_T, 1)
                    for i in range(PRE, AHEAD):
                        for k in range(KC):
                            u, g = k % 2, (i - PRE) * KC + k
                            pe.wait_ge(oh_ready, b * (P // 4) + (g + 1))
                            pe.wait_ge(g_cp, b * (P // 4) + (g + 1))
                            for r in range(4):
                                last = pe.matmul(t.psum[:, 4 + u, r * P:(r + 1) * P], oi[:, 4 * u + r],
                                                 oj[:, 4 * u + r], start=True, stop=True)
                            last.then_inc(g_mm, 1)
                            up(b * AHEAD + i, i, [k])

            @block.scalar
            def _(act):
                for x in range(2):
                    act.sem_inc(stored[x], 16)

                def ahead(b, i):
                    c = b * AHEAD + i
                    t.wait_product(act, c)
                    act.wait_ge(spilled[i % 2], b * (16 * AHEAD // 2) + 16 * (i // 2 + 1))
                    act.activation(split_tokens(act_f[:, i % 2], tokens), t.acc(i % SPLIT, tokens),
                                   ACT.Gelu).then_inc(gelu_done, 1)
                    act.wait_ge(gelu_done, c + 1)
                    act.sem_inc(t.acc_free[i % SPLIT], 1)
                    t.hi(act, c + SPLIT, (i + SPLIT) % RAW, i % SPLIT, b * (AHEAD // RAW) + (i + SPLIT) // RAW)
                for x in range(2):
                    act.sem_inc(spilled[x], 16)
                for i in range(SPLIT):
                    t.hi(act, i, i, i, 0)
                with act.Fori(0, blocks) as b:
                    for i in range(PRE):
                        ahead(b, i)
                        if i == PRE // 2 - 1:
                            act.wait_ge(ex_in, b + 1)
                            act.activation(ex[:], ex[:], ACT.Exp).then_inc(ex_done, 1)
                    for s in range(STAGES):
                        act.wait_ge(stored[s % 2], b * (16 * STAGES // 2) + 16 * (s // 2 + 1))
                        with act.Fori(0, STEPS_S) as q:
                            for u in range(2):
                                act.wait_ge(g_mm, b * (P // 4) + q * 2 + (s * (STAGE_T // 4) + u + 3))
                                act.activation(stage[:, s % 2, :, bass.ds(q * 8 + 4 * u, 4)],
                                               t.psum[:, 4 + u, :].rearrange("p (t j) -> p j t", j=NKEYS),
                                               ACT.Copy).then_inc(g_cp, 1)
                        ahead(b, PRE + s)

            @block.gpsimd
            def _(pool):
                for i in range(SPLIT):
                    t.lo(pool, i, i, i)
                with pool.Fori(0, blocks) as b:
                    for i in range(AHEAD):
                        t.lo(pool, b * AHEAD + (i + SPLIT), (i + SPLIT) % RAW, i % SPLIT)

            @block.sync
            def _(sp):
                def load(c, i):
                    t.load(sp, t.a[f"peer_u{layer}"][bass.ds(c, 1)].rearrange("a p n -> p (a n)"),
                           c, i % RAW, RAW, None)

                def ahead(b, i):
                    sp.wait_ge(gelu_done, b * AHEAD + (i + 1))
                    sp.dma_start(act_dram[bass.ds(b * AHEAD + i, 1)].rearrange("a p x -> p (a x)"),
                                 act_f[:, i % 2]).then_inc(spilled[i % 2], 16)
                    load(b * AHEAD + (i + RAW), i)
                for i in range(RAW):
                    load(i, i)
                with sp.Fori(0, blocks) as b:
                    for i in range(PRE):
                        ahead(b, i)
                    for s in range(STAGES):
                        sp.wait_ge(g_cp, b * (P // 4) + ((s + 1) * (STAGE_T // 4) + 2))
                        sp.dma_start(
                            g_dram.rearrange("g i n x -> n i g x")[bass.ds(b * STAGES + s, 1)].rearrange(
                                "a i g x -> i (a g) x"),
                            stage[:, s % 2].rearrange("p (g j) t -> p g (j t)", j=QUAD)).then_inc(stored[s % 2], 16)
                        ahead(b, PRE + s)
                for x in range(2):
                    sp.wait_ge(spilled[x], 16 * (blocks * AHEAD // 2 + 1))
                    sp.wait_ge(stored[x], 16 * (blocks * STAGES // 2 + 1))


def stage_experts(t, layer, tokens, g_dram, act_dram):
    nc = t.nc
    T = tokens
    segs = [(0, SEQ, 0)] + ([(SEQ, CTX, 1)] if tokens == TOK else [])
    NT = KC * len(segs)
    tag = f"e{layer}"
    n = NKEYS
    R = AHEAD * tokens // P
    QR = R // QUAD
    with ExitStack() as ctx:
        sb = lambda nm, s, d=F32: ctx.enter_context(nc.sbuf_tensor(nm + tag, s, d))
        act_in = [t.sem(f"act_in{x}{tag}") for x in range(2)]
        gt = sb("gt", [P, 2, QUAD * T])
        act_f = sb("act_f", [P, 2, T])
        a_hi = sb("a_hi", [P, 4, T], F32R)
        a_lo = sb("a_lo", [P, 4, T], F32R)
        vr = sb("v_raw", [P, 2, D])
        v_hi = sb("v_hi", [P, 4, D], F32R)
        v_lo = sb("v_lo", [P, 4, D], F32R)
        g_in, gelu_done, gated, ahi_done, alo_done = (
            t.sem(x + tag) for x in ("g_in", "gelu_done", "gated", "ahi_done", "alo_done"))
        act_free = t.sem("act_free" + tag)
        v_in = [t.sem(f"v_in{x}{tag}") for x in range(2)]
        vhi_done, vlo_done, out_mm, out_free, pair_done = (
            t.sem(x + tag) for x in ("vhi_done", "vlo_done", "out_mm", "out_free", "pair_done"))
        with nc.Block() as block:

            @block.sync
            def _(sp):
                sp.sem_inc(g_in, 1)

                def u_load(c, i, turn):
                    t.load(sp, t.a[f"peer_u{layer}"][bass.ds(c, 1)].rearrange("a p n -> p (a n)"),
                           c, i, RAW, turn)

                def quad(q, stored, more):
                    sp.wait_ge(g_in, q * 16 + 1)
                    sp.wait_ge(gated, q * QUAD + 1)
                    sp.dma_start(gt[:, bass.ds(q % 2, 1), :].rearrange("p a x -> p (a x)"),
                                 g_dram[bass.ds(q, 1)].rearrange("a i n x -> i (a n x)")).then_inc(g_in, 16)
                    for i in range(QUAD):
                        c = q * QUAD + i
                        if stored:
                            sp.wait_ge(act_free, c + 1)
                            sp.dma_start(act_f[:, i % 2], act_dram[bass.ds(c, 1)].rearrange(
                                "a p x -> p (a x)")).then_inc(act_in[i % 2], 16)
                        elif more:
                            u_load(c + RAW, i, None)
                        sp.wait_ge(vlo_done, c + 1)
                        sp.dma_start(vr[:, i % 2, :], t.a[f"peer_v{layer}"][bass.ds(c, 1)].rearrange(
                            "a p n -> p (a n)")).then_inc(v_in[i % 2], 16)
                with sp.Fori(0, QR) as q:
                    quad(q, True, False)
                with sp.Fori(QR, n // QUAD - 1) as q:
                    quad(q, False, True)
                quad(n // QUAD - 1, False, False)

            @block.gpsimd
            def _(pool):
                pool.sem_inc(vlo_done, 2)

                def v_low(c, i):
                    pool.wait_ge(vhi_done, c + 1)
                    pool.tensor_tensor(v_lo[:, i], vr[:, i % 2], v_hi[:, i].bitcast(F32),
                                       ALU.subtract).then_inc(vlo_done, 1)
                with pool.Fori(0, QR) as q:
                    for i in range(QUAD):
                        v_low(q * QUAD + i, i)
                with pool.Fori(QR, n // QUAD - 1) as q:
                    for i in range(QUAD):
                        t.lo(pool, q * QUAD + (i + SPLIT), (i + SPLIT) % RAW, i % SPLIT)
                        v_low(q * QUAD + i, i)
                for i in range(QUAD):
                    if i + SPLIT < QUAD:
                        t.lo(pool, n - QUAD + i + SPLIT, i + SPLIT, i % SPLIT)
                    v_low(n - QUAD + i, i)

            @block.tensor
            def _(pe):
                def pair(p, odd):
                    pe.wait_ge(alo_done, p * 2 + 2)
                    pe.wait_ge(vlo_done, p * 2 + 4)
                    for m in range(NT):
                        d, (t0, w, _) = m // len(segs), segs[m % len(segs)]
                        pe.wait_ge(out_free, p * NT + (m + 1))
                        for j in range(2):
                            sl = 2 * odd + j
                            vh, vl = (v[:, sl, d * P:(d + 1) * P] for v in (v_hi, v_lo))
                            out = t.psum[:, 4 + m % 4, 0:w]
                            pe.matmul(out, vh, a_hi[:, sl, t0:t0 + w], start=(j == 0), stop=False)
                            pe.matmul(out, vh, a_lo[:, sl, t0:t0 + w], start=False, stop=False)
                            last = pe.matmul(out, vl, a_hi[:, sl, t0:t0 + w], start=False, stop=(j == 1))
                        last.then_inc(out_mm, 1)
                up = lambda c, s: t.product(pe, c, s, T, t.h_hi, t.h_lo)
                pe.sem_inc(out_free, 4)
                with pe.Fori(0, QR - 1) as q:
                    for m in range(2):
                        pair(q * 2 + m, m)
                pair(R // 2 - 2, 0)
                up(R, 0)
                up(R + 1, 1)
                pair(R // 2 - 1, 1)
                with pe.Fori(QR, n // QUAD - 1) as q:
                    for m in range(2):
                        up(q * QUAD + (2 * m + 2), 0)
                        up(q * QUAD + (2 * m + 3), 1)
                        pair(q * 2 + m, m)
                up(n - 2, 0)
                up(n - 1, 1)
                pair(n // 2 - 2, 0)
                pair(n // 2 - 1, 1)

            @block.scalar
            def _(act):
                def chunk(c, i, stored, turn):
                    if not stored:
                        t.wait_product(act, c)
                        act.wait_ge(act_free, c + 1)
                        act.activation(split_tokens(act_f[:, i % 2], T), t.acc(i % 2, T),
                                       ACT.Gelu).then_inc(gelu_done, 1)
                        act.wait_ge(gelu_done, c - (R - 1))
                        act.sem_inc(t.acc_free[i % SPLIT], 1)
                    if turn is not None:
                        t.hi(act, c + SPLIT, (i + SPLIT) % RAW, i % SPLIT, turn)
                    act.wait_ge(v_in[i % 2], vturn(c, i))
                    act.wait_ge(pair_done, turn_q * 2 + (i // 2 + 1))
                    act.activation(v_hi[:, i, :], vr[:, i % 2, :], ACT.Copy).then_inc(vhi_done, 1)
                    act.wait_ge(gated, c + 6)
                    act.activation(a_hi[:, i, :], act_f[:, i % 2], ACT.Copy).then_inc(ahi_done, 1)
                act.sem_inc(act_free, 2)
                act.sem_inc(pair_done, 2)
                vturn = lambda c, i: turn_q * 32 + 16 * (i // 2 + 1)
                with act.Fori(0, QR) as q:
                    turn_q = q
                    for i in range(QUAD):
                        chunk(q * QUAD + i, i, True, None)
                with act.Fori(QR, n // QUAD - 1) as q:
                    turn_q = q
                    for i in range(QUAD):
                        chunk(q * QUAD + i, i, False, q + (i + SPLIT) // RAW)
                turn_q = n // QUAD - 1
                for i in range(QUAD):
                    chunk(n - QUAD + i, i, False, turn_q if i + SPLIT < QUAD else None)

            @block.vector
            def _(dve):
                def chunk(q, i, stored):
                    c = q * QUAD + i
                    if stored:
                        dve.wait_ge(act_in[i % 2], q * 32 + 16 * (i // 2 + 1))
                    else:
                        dve.wait_ge(gelu_done, c - (R - 1))
                    if i == 0:
                        dve.wait_ge(g_in, q * 16 + 17)
                    g = gt[:, bass.ds(q % 2, 1), :].rearrange("p a (n j t) -> p j (a n) t", j=QUAD, t=STAGE_T)[:, i]
                    a = act_f[:, i % 2].rearrange("p (n t) -> p n t", t=STAGE_T)
                    dve.tensor_tensor(a, a, g, ALU.mult).then_inc(gated, 1)
                    dve.wait_ge(ahi_done, c + 1)
                    dve.tensor_tensor(a_lo[:, i], act_f[:, i % 2], a_hi[:, i].bitcast(F32), ALU.subtract).then_inc(alo_done, 1)
                    dve.wait_ge(alo_done, c + 1)
                    dve.sem_inc(act_free, 1)

                def gather(p, part=None):
                    for m in range(NT) if part is None else range(part * NT // 2, (part + 1) * NT // 2):
                        d, (t0, w, cond) = m // len(segs), segs[m % len(segs)]
                        dve.wait_ge(out_mm, p * NT + (m + 1))
                        x = t.xT[:, d, t0:t0 + w]
                        dve.scalar_tensor_tensor(out=x, in0=t.psum[:, 4 + m % 4, 0:w],
                                                 scalar=t.mod[:, layer, cond, 40 + d:41 + d], in1=x,
                                                 op0=ALU.mult, op1=ALU.add).then_inc(out_free, 1)
                    if part != 0:
                        dve.wait_ge(out_free, p * NT + (NT + 4))
                        dve.sem_inc(pair_done, 1)
                dve.sem_inc(gated, 5)
                for i in range(QUAD):
                    chunk(0, i, True)
                    if i >= 2:
                        gather(0, i - 2)
                with dve.Fori(1, QR) as q:
                    for i in range(QUAD):
                        chunk(q, i, True)
                        gather(q * 2 + (i // 2 - 1), i % 2)
                with dve.Fori(QR, n // QUAD) as q:
                    for i in range(QUAD):
                        if i % 2:
                            gather(q * 2 + (i // 2 - 1))
                        chunk(q, i, False)
                gather(n // 2 - 1)
        t.end_stage(n, RAW)


def stage_hgrn(t, y):
    nc = t.nc
    n, PER, BODY, N_RAW = 5 * HEADS, 5, 10, 2
    LAYER = 1
    MID = (CHUNK // 2, CHUNK - 1 - CHUNK // 2)
    LAST = (CHUNK - 1, 0)
    ORDER = ([XCH + c for c in range(CCH)] + list(range(XCH)),
             [XCH + CCH - 1 - c for c in range(CCH)] + [XCH - 1 - c for c in range(XCH)])
    KV = [(s, d) for s in range(NCH - 1) for d in range(2)]
    ROWS = P // CHUNK
    KVG = [KV[i:i + 2 * ROWS] for i in range(0, len(KV), 2 * ROWS)]
    BLOCK = [[ORDER[d][ROWS * x] // ROWS for x in range(NCH // ROWS)] for d in range(2)]
    BLK = TOK // P
    with ExitStack() as ctx:
        sb = lambda nm, s, d=F32: ctx.enter_context(nc.sbuf_tensor(nm, s, d))
        f = [sb(f"f{d}", [P, TOK]) for d in range(2)]
        kk = [sb(f"kk{d}", [P, TOK]) for d in range(2)]
        b = [sb(f"b{d}", [P, TOK]) for d in range(2)]
        e = [sb(f"e{d}", [P, TOK]) for d in range(2)]
        qm = [sb(f"qm{d}", [P, SEQ]) for d in range(2)]
        km = [sb(f"km{d}", [P, SEQ]) for d in range(2)]
        qd = [sb(f"qd{d}", [P, SEQ]) for d in range(2)]
        dc = [sb(f"dc{d}", [P, NCH]) for d in range(2)]
        reset = sb("reset", [P, TOK])
        vT, qs, zs = sb("vT", [P, TOK]), sb("qs", [P, SEQ]), sb("zs", [P, SEQ])
        v_tok = sb("v_tok", [P, BLK, P])
        v_by_chunk = sb("v_by_chunk", [P, BLK, ROWS, P])
        kd_tok = [sb(f"kd_tok{d}", [P, BLK, P]) for d in range(2)]
        probs = [sb(f"probs{d}", [P, SEQ]) for d in range(2)]
        same = [sb(f"same{d}", [P, P]) for d in range(2)]
        state = [t.raw[:, N_RAW:RAW].rearrange("p a (c x) -> p (a c) x", x=P), sb("state1", [P, XCH, P])]
        names = ("reset_done", "mask_done", "f_in", "v_in", "q_in", "z_in", "f_done", "k_done", "ln_done", "b_done",
                 "d1", "d1_exp", "m_done", "d2", "d2_exp", "kd_done", "b_exp", "qd_done", "dc_done",
                 "tok_mm", "tok_cp", "score_mm", "prob_done", "kv_mm", "st_done", "kv_free", "o_mm", "o_cp",
                 "osq", "osum", "oroot", "orstd", "on", "y_done", "vc_part", "vc_done")
        S = {x: t.sem("h_" + x) for x in names}
        xv = lambda ap: ap[:, 0:SEQ].rearrange("p (c l) -> p c l", l=CHUNK)
        av = lambda ap: ap[:].rearrange("p (c l) -> p c l", l=CHUNK)
        o = e[0][:, 0:SEQ]
        osq = e[1][:, 0:SEQ]
        orn = b[0][:, 0:SEQ]
        ony = b[1][:, 0:SEQ]
        with nc.Block() as block:

            @block.sync
            def _(sp):
                with sp.Fori(0, n // BODY) as q:
                    for i in range(BODY):
                        t.load(sp, t.a["hgrn_w_in"][bass.ds(q * BODY + i, 1)].rearrange("a p n -> p (a n)"),
                               q * BODY + i, i % N_RAW, N_RAW, None)

            @block.gpsimd
            def _(pool):
                pool.memset(reset[:], 1.0).then_inc(S["reset_done"], 1)
                for d in range(2):
                    pool.memset(same[d][:], 1.0).then_inc(S["mask_done"], 1)
                    pool.memset(probs[d][:], 0.0).then_inc(S["reset_done"], 1)
                pool.wait_ge(S["reset_done"], 3)
                pool.memset(av(reset)[:, :, 0:1], 0.0).then_inc(S["reset_done"], 1)
                m = 2
                for d in range(2):
                    sv = same[d][:].rearrange("p (c l) -> p c l", l=CHUNK)
                    sign = 1 if d == 0 else -1
                    pool.wait_ge(S["mask_done"], m)
                    pool.affine_select(out=sv, in_=sv, compare_op=ALU.is_ge, fill=0.0, base=0,
                                       pattern=[[sign * CHUNK, P // CHUNK], [sign, CHUNK]],
                                       channel_multiplier=-sign).then_inc(S["mask_done"], 1)
                    m += 1
                    pool.wait_ge(S["mask_done"], m)
                    pool.affine_select(out=sv, in_=sv, compare_op=ALU.is_ge, fill=0.0,
                                       base=0 if d == 0 else CHUNK - 1,
                                       pattern=[[-sign * CHUNK, P // CHUNK], [0, CHUNK]],
                                       channel_multiplier=sign).then_inc(S["mask_done"], 1)
                    m += 1
                pool.memset(v_by_chunk[:], 0.0).then_inc(S["vc_part"], 1)
                with pool.Fori(0, HEADS // 2) as q:
                    for u in range(2):
                        h = q * 2 + u
                        for i in range(PER * u, PER * (u + 1)):
                            t.lo(pool, q * BODY + i, i % N_RAW, i % SPLIT)
                        pool.wait_ge(S["vc_part"], h * ROWS + 1)
                        pool.wait_ge(S["tok_cp"], h * 3 + 2)
                        t.settle(pool)
                        for r in range(ROWS):
                            rows = slice(r * CHUNK, (r + 1) * CHUNK)
                            pool.tensor_copy(v_by_chunk[rows, :, r], v_tok[rows]).then_inc(S["vc_part"], 1)
                        pool.wait_ge(S["vc_part"], h * ROWS + (ROWS + 1))
                        pool.sem_inc(S["vc_done"], 1)

            @block.tensor
            def _(pe):
                def bank(x):
                    return t.psum[:, 4 + x]

                def head(h, i0):
                    for i in range(PER):
                        t.product(pe, h * PER + i, (i0 + i) % SPLIT, TOK if i < 3 else SEQ, t.h_hi, t.h_lo)
                    srcs = (vT, kk[0], kk[1])
                    for x, src in enumerate(srcs):
                        if x == 0:
                            pe.wait_ge(S["v_in"], h + 1)
                        else:
                            pe.wait_ge(S["kd_done"], h * 2 + x)
                        pe.wait_ge(S["tok_cp"], h * 3 + (x + 1))
                        for g in range(BLK):
                            last = pe.transpose(bank(g // 4)[:, (g % 4) * P:(g % 4 + 1) * P],
                                                src[:, g * P:(g + 1) * P], t.ident[:])
                        last.then_inc(S["tok_mm"], 1)
                    for d in range(2):
                        pe.wait_ge(S["m_done"], h * 4 + 2 * d + 2)
                        pe.wait_ge(S["prob_done"], h * 2 + d + 1)
                        for g in range(SEQ // P):
                            sl = slice(g * P, (g + 1) * P)
                            last = pe.matmul(bank(2)[:, sl], km[d][:, sl], qm[d][:, sl], start=True, stop=True)
                        last.then_inc(S["score_mm"], 1)
                    pe.wait_ge(S["tok_cp"], h * 3 + 4)
                    pe.wait_ge(S["vc_done"], h + 1)
                    pe.wait_ge(S["prob_done"], h * 2 + 3)
                    pe.wait_ge(S["o_cp"], h + 1)
                    for x, grp in enumerate(KVG):
                        pe.wait_ge(S["kv_free"], h * len(KVG) + (x + 1))
                        for d in range(2):
                            g = BLOCK[d][x]
                            last = pe.matmul(bank(2 * d + x % 2), kd_tok[d][:, g],
                                             v_by_chunk[:, g].rearrange("p r x -> p (r x)"),
                                             start=True, stop=True)
                        last.then_inc(S["kv_mm"], 1)
                    pe.wait_ge(S["st_done"], h * len(KV) + len(KV))
                    for d in range(2):
                        for g in range(SEQ // P):
                            sl = slice(g * P, (g + 1) * P)
                            pe.matmul(bank(3)[:, sl], v_tok[:, g], probs[d][:, sl],
                                      start=(d == 0 and g == 0), stop=False, skip_group_check=True)
                    pe.wait_ge(S["qd_done"], h * 2 + 2)
                    for d in range(2):
                        for c in range(XCH):
                            sl = slice(c * CHUNK, (c + 1) * CHUNK)
                            last = pe.matmul(bank(3)[:, sl], state[d][:, c], qd[d][:, sl], start=False,
                                             stop=(d == 1 and c == XCH - 1), skip_group_check=True)
                    last.then_inc(S["o_mm"], 1)
                    pe.wait_ge(S["osq"], h + 1)
                    pe.matmul(bank(2), t.ones[:], osq, start=True, stop=True).then_inc(S["osum"], 1)
                for x in ("tok_cp", "prob_done", "o_cp"):
                    pe.sem_inc(S[x], 1)
                pe.sem_inc(S["kv_free"], 2)
                with pe.Fori(0, HEADS // 2) as q:
                    for u in range(2):
                        head(q * 2 + u, PER * u)

            @block.scalar
            def _(act):
                def head(q, u):
                    h = q * 2 + u
                    for i in range(PER):
                        j = PER * u + i
                        t.hi(act, q * BODY + j, j % N_RAW, j % SPLIT, q * (BODY // N_RAW) + j // N_RAW)
                        if i == 0:
                            act.wait_ge(S["y_done"], h + 1)
                        else:
                            evac(q, u, i - 1)
                    evac(q, u, PER - 1)
                    for d in range(2):
                        act.wait_ge(S["k_done"], h * 2 + d + 1)
                        act.activation(f[d][:], f[d][:], ACT.Ln).then_inc(S["ln_done"], 1)
                    for d in range(2):
                        act.wait_ge(S["b_done"], h * 2 + d + 1)
                        act.activation(qd[d][:], b[d][:, 0:SEQ], ACT.Exp).then_inc(S["b_exp"], 1)
                        act.activation(dc[d][:].unsqueeze(2), av(b[d])[:, :, LAST[d]:LAST[d] + 1],
                                       ACT.Exp).then_inc(S["dc_done"], 1)
                        act.wait_ge(S["d2"], h * 2 + d + 1)
                        act.activation(e[d][:], e[d][:], ACT.Exp).then_inc(S["d2_exp"], 1)
                        act.wait_ge(S["d1"], h * 2 + d + 1)
                        act.activation(km[d][:], qm[d][:], ACT.Exp, scale=-1.0).then_inc(S["d1_exp"], 1)
                        act.wait_ge(S["d1_exp"], h * 4 + 2 * d + 1)
                        act.activation(qm[d][:], qm[d][:], ACT.Exp).then_inc(S["d1_exp"], 1)
                    dsts = (v_tok, kd_tok[0], kd_tok[1])
                    for x, dst in enumerate(dsts):
                        act.wait_ge(S["tok_mm"], h * 3 + x + 1)
                        for g0, g1 in ((0, 4), (4, BLK)):
                            last = act.activation(dst[:, g0:g1], t.psum[:, 4 + g0 // 4, 0:(g1 - g0) * P].rearrange(
                                "p (g x) -> p g x", x=P), ACT.Copy)
                        last.then_inc(S["tok_cp"], 1)
                    act.wait_ge(S["o_mm"], h + 1)
                    act.activation(o, t.psum[:, 7], ACT.Copy).then_inc(S["o_cp"], 1)
                    act.wait_ge(S["o_cp"], h + 2)
                    act.activation(osq, o, ACT.Square).then_inc(S["osq"], 1)
                    act.wait_ge(S["osum"], h + 1)
                    act.activation(orn, t.psum[:, 6], ACT.Sqrt, bias=t.eps[:], scale=1.0 / P).then_inc(S["oroot"], 1)

                def evac(q, u, i):
                    j = PER * u + i
                    h = q * 2 + u
                    t.wait_product(act, q * BODY + j)
                    T = TOK if i < 3 else SEQ
                    dst = (f[0], f[1], vT, qs, zs)[i][:, 0:T]
                    func = (ACT.Sigmoid, ACT.Sigmoid, ACT.Copy, ACT.Silu, ACT.Silu)[i]
                    name = ("f_in", "f_in", "v_in", "q_in", "z_in")[i]
                    act.activation(split_tokens(dst, T), t.acc(j % SPLIT, T), func).then_inc(S[name], 1)
                    act.wait_ge(S[name], h * 2 + i + 1 if i < 2 else h + 1)
                    act.sem_inc(t.acc_free[j % SPLIT], 1)
                act.sem_inc(S["y_done"], 1)
                with act.Fori(0, HEADS // 2) as q:
                    for u in range(2):
                        head(q, u)

            @block.vector
            def _(dve):
                bcl = lambda ap, c: ap.to_broadcast([P, c, CHUNK])

                def head(h):
                    hs = lambda ap: ap[:, bass.ds(h, 1)]
                    for d in range(2):
                        dve.wait_ge(S["f_in"], h * 2 + d + 1)
                        dve.tensor_scalar(f[d][:], f[d][:], hs(t.lb[:, 1, d]), hs(t.lb[:, 0, d]), ALU.mult,
                                          ALU.add).then_inc(S["f_done"], 1)
                        dve.wait_ge(S["f_done"], h * 2 + d + 1)
                        dve.tensor_scalar(kk[d][:], f[d][:], -1.0, 1.0, ALU.mult, ALU.add).then_inc(S["k_done"], 1)
                    for d in range(2):
                        dve.wait_ge(S["ln_done"], h * 2 + d + 1)
                        w = slice(None) if d == 0 else slice(None, None, -1)
                        dve.tensor_tensor_scan(b[d][:, w], reset[:], f[d][:, w], 0.0, ALU.mult,
                                               ALU.add).then_inc(S["b_done"], 1)
                    dve.wait_ge(S["q_in"], h + 1)
                    for d in range(2):
                        dve.wait_ge(S["b_done"], h * 2 + d + 1)
                        dve.tensor_tensor(av(e[d]), bcl(av(b[d])[:, :, LAST[d]:LAST[d] + 1], NCH), av(b[d]),
                                          ALU.subtract).then_inc(S["d2"], 1)
                        dve.tensor_tensor(xv(qm[d]), xv(b[d]), bcl(xv(b[d])[:, :, MID[d]:MID[d] + 1], XCH),
                                          ALU.subtract).then_inc(S["d1"], 1)
                        dve.wait_ge(S["d1_exp"], h * 4 + 2 * d + 2)
                        dve.tensor_tensor(km[d][:], km[d][:], kk[d][:, 0:SEQ], ALU.mult).then_inc(S["m_done"], 1)
                        dve.tensor_tensor(qm[d][:], qm[d][:], qs[:], ALU.mult).then_inc(S["m_done"], 1)
                        dve.wait_ge(S["d2_exp"], h * 2 + d + 1)
                        dve.wait_ge(S["m_done"], h * 4 + 2 * d + 1)
                        dve.tensor_tensor(kk[d][:], kk[d][:], e[d][:], ALU.mult).then_inc(S["kd_done"], 1)
                        dve.wait_ge(S["b_exp"], h * 2 + d + 1)
                        dve.tensor_tensor(qd[d][:], qd[d][:], qs[:], ALU.mult).then_inc(S["qd_done"], 1)
                    dve.wait_ge(S["mask_done"], 6)
                    for d in range(2):
                        dve.wait_ge(S["score_mm"], h * 2 + d + 1)
                        t.settle(dve)
                        dve.copy_predicated(probs[d][:].rearrange("p (g l) -> p g l", l=P),
                                            same[d][:].bitcast(U32).unsqueeze(1).to_broadcast([P, SEQ // P, P]),
                                            t.psum[:, 6].rearrange("p (g l) -> p g l", l=P)).then_inc(S["prob_done"], 1)
                    dve.wait_ge(S["dc_done"], h * 2 + 2)
                    at = 0
                    for x, grp in enumerate(KVG):
                        dve.wait_ge(S["kv_mm"], h * len(KVG) + x + 1)
                        for s, d in grp:
                            c = ORDER[d][s]
                            r = c % ROWS
                            kv = t.psum[:, 4 + 2 * d + x % 2, r * P:(r + 1) * P]
                            dst = state[d][:, ORDER[d][max(s + 1, CCH)]]
                            if s == 0:
                                ins = dve.tensor_copy(dst, kv)
                            else:
                                dve.wait_ge(S["st_done"], h * len(KV) + at - 1)
                                ins = dve.scalar_tensor_tensor(
                                    out=dst, in0=state[d][:, ORDER[d][max(s, CCH)]], scalar=dc[d][:, c:c + 1],
                                    in1=kv, op0=ALU.mult, op1=ALU.add)
                            ins.then_inc(S["st_done"], 1)
                            at += 1
                        dve.wait_ge(S["st_done"], h * len(KV) + at)
                        dve.sem_inc(S["kv_free"], 1)
                    dve.wait_ge(S["oroot"], h + 1)
                    dve.reciprocal(orn, orn).then_inc(S["on"], 1)
                    dve.wait_ge(S["on"], h * 2 + 1)
                    dve.tensor_tensor(ony, o, orn, ALU.mult).then_inc(S["on"], 1)
                    dve.wait_ge(S["on"], h * 2 + 2)
                    dve.wait_ge(S["z_in"], h + 1)
                    dve.scalar_tensor_tensor(out=y[:, bass.ds(h, 1)].rearrange("p a n -> p (a n)"), in0=ony,
                                             scalar=hs(t.gains[:, 5]), in1=zs[:], op0=ALU.mult,
                                             op1=ALU.mult).then_inc(S["y_done"], 1)
                    dve.wait_ge(S["y_done"], h + 2)
                dve.wait_ge(S["reset_done"], 4)
                with dve.Fori(0, HEADS // 2) as q:
                    for u in range(2):
                        head(q * 2 + u)
        t.end_stage(n, N_RAW)


def stage_split(t, y):
    nc = t.nc
    hi_done, lo_done = t.sem("y_hi_done"), t.sem("y_lo_done")
    with nc.Block() as block:

        @block.scalar
        def _(act):
            for k in range(KC):
                act.activation(t.h_hi[:, k, 0:SEQ], y[:, k], ACT.Copy).then_inc(hi_done, 1)

        @block.vector
        def _(dve):
            for k in range(KC):
                dve.wait_ge(hi_done, k + 1)
                dve.tensor_tensor(t.h_lo[:, k, 0:SEQ], y[:, k], t.h_hi[:, k, 0:SEQ].bitcast(F32),
                                  ALU.subtract).then_inc(lo_done, 1)
            dve.wait_ge(lo_done, KC)


def hybrid_trunk(nc, a):
    with ExitStack() as ctx:
        t = Trunk(nc, ctx, a)
        g_dram = [nc.dram_tensor(f"gates{i}", [GROUPS, P, T // STAGE_T, QUAD * STAGE_T], F32, kind="Internal").ap()
                  for i, T in enumerate((TOK, SEQ))]
        act_dram = [nc.dram_tensor(f"acts{i}", [AHEAD * T // P, P, T], F32, kind="Internal").ap()
                    for i, T in enumerate((TOK, SEQ))]
        stage_setup(t)
        t.retire()
        for layer, tokens in enumerate((TOK, SEQ)):
            stage_norm(t, layer, 0, TOK)
            t.retire()
            with ExitStack() as mix:
                if layer == 0:
                    y_hi = mix.enter_context(nc.sbuf_tensor("y_hi", [P, KC, TOK], F32R))
                    y_lo = mix.enter_context(nc.sbuf_tensor("y_lo", [P, KC, TOK], F32R))
                    stage_conv(t, y_hi, y_lo)
                    t.retire()
                    stage_mix_out(t, layer, "conv_w_out", tokens, y_hi, y_lo)
                    t.retire()
                else:
                    y = mix.enter_context(nc.sbuf_tensor("y_heads", [P, KC, SEQ], F32))
                    stage_hgrn(t, y)
                    t.retire()
                    stage_split(t, y)
                    t.retire()
                    stage_mix_out(t, layer, "hgrn_w_out", tokens, t.h_hi, t.h_lo)
                    t.retire()
            stage_norm(t, layer, 1, tokens)
            t.retire()
            with ExitStack() as pick:
                top = pick.enter_context(nc.sbuf_tensor(f"top{layer}", [P, tokens // P, LISTS, TOPK], F32))
                top_i = pick.enter_context(nc.sbuf_tensor(f"top_i{layer}", [P, tokens // P, LISTS, TOPK], U32))
                stage_rank(t, layer, tokens, top, top_i)
                t.retire()
                stage_gates(t, layer, tokens, top, top_i, g_dram[layer], act_dram[layer])
                t.retire()
            stage_experts(t, layer, tokens, g_dram[layer], act_dram[layer])
            t.retire()
        stage_norm(t, 1, 2, SEQ)
        t.retire()


def kernel(**inputs):
    import numpy as np
    import concourse.bacc as bacc
    from concourse.bass_utils import run_bass_kernel_spmd

    i = {k: np.asarray(v) for k, v in inputs.items()}

    def cols(v):
        v = v.reshape(v.shape[:-1] + (-1, P))
        return np.moveaxis(v, -1, 0)

    def tiles(w):
        k, m = w.shape
        return w.reshape(k // P, P, m // P, P).transpose(2, 1, 0, 3).reshape(m // P, P, k)

    def grouped(w, order):
        tl = tiles(w).reshape(-1, KC, P, D)
        return tl[order].transpose(1, 0, 2, 3).reshape(-1, P, D)

    send = {
        "x": i["x"][0].T.reshape(KC, P, SEQ).transpose(1, 0, 2),
        "ctx": i["ctx"][0].T.reshape(KC, P, CTX).transpose(1, 0, 2),
        "cond": np.stack([cols(i["c"][0]), cols(i["c_ctx"])], axis=-1),
        "ada_w": i["ada_w"].reshape(2, KC, P, 12, 512).transpose(0, 3, 2, 1, 4).reshape(24, P, KC, 512),
        "ada_b": cols(i["ada_b"]),
        "gains": cols(np.stack([i["norm1_g"][0], i["norm1_g"][1], i["norm2_g"][0], i["norm2_g"][1],
                                i["final_g"], i["hgrn_norm_g"][0]])),
        "hgrn_lb": cols(i["hgrn_lb"]),
        "conv_w_in": grouped(i["conv_w_in"][0], [1, 2, 0]),
        "conv_k": cols(i["conv_k"][0]).transpose(0, 2, 1),
        "conv_w_out": tiles(i["conv_w_out"][0]),
        "hgrn_w_in": grouped(i["hgrn_w_in"][0], [2, 3, 1, 0, 4]),
        "hgrn_w_out": tiles(i["hgrn_w_out"][0]),
        "peer_keys": i["peer_keys"].reshape(2, LISTS, NKEYS, P).transpose(0, 3, 1, 2),
    }
    for n in range(2):
        send[f"peer_w_q{n}"] = tiles(i["peer_w_q"][n])
        u = i["peer_u"][n].reshape(NKEYS, NKEYS, KC, P)
        send[f"peer_u{n}"] = u.transpose(1, 3, 2, 0).reshape(NKEYS, P, D)
        send[f"peer_v{n}"] = i["peer_v"][n].reshape(NKEYS, NKEYS, D).transpose(1, 0, 2)
    send = {k: np.ascontiguousarray(v) for k, v in send.items()}

    nc = bacc.Bacc("TRN2", target_bir_lowering=False, num_devices=1)
    a = {k: nc.dram_tensor("in_" + k, v.shape, mybir.dt.from_np(v.dtype), kind="ExternalInput").ap()
         for k, v in send.items()}
    a["out"] = nc.dram_tensor("out_x", (P, KC, SEQ), F32, kind="ExternalOutput").ap()
    hybrid_trunk(nc, a)
    r = run_bass_kernel_spmd(nc, [{"in_" + k: v for k, v in send.items()}], core_ids=[0])
    out = r.results[0]["out_x"]
    return np.ascontiguousarray(out.transpose(2, 1, 0)).reshape(1, SEQ, D)
```

```python
from contextlib import ExitStack

import concourse.bass as bass
from concourse import mybir
from concourse.alu_op_type import AluOpType as ALU

ACT = mybir.ActivationFunctionType
AX = mybir.AxisListType
F32 = mybir.dt.float32
F32R = mybir.dt.float32r
U32 = mybir.dt.uint32

P = 128
D = 1024
KC = D // P
SEQ, CTX = 512, 256
TOK = SEQ + CTX
GRID_W = 64
HEADS = 8
TOPK = 16
NKEYS = 128
LISTS = 2 * HEADS
CHUNK = 32
XCH = SEQ // CHUNK
CCH = CTX // CHUNK
NCH = XCH + CCH
EPS = 1e-6
LOWEST = -3.0e38
RAW = 4
SPLIT = 2
STAGE_T = 32
QUAD = 4
GROUPS = NKEYS // QUAD
AHEAD = (8, 12)


def halves(tokens):
    n = 1 if tokens <= 512 else 2
    return [(i * tokens // n, tokens // n) for i in range(n)]


class Trunk:

    def __init__(self, nc, ctx, a):
        self.nc, self.a = nc, a

        def sb(name, shape, dt=F32):
            return ctx.enter_context(nc.sbuf_tensor(name, shape, dt))

        def sem(name):
            return ctx.enter_context(nc.semaphore(name))

        self.own = []
        self.own_ctx = ExitStack()
        self.xT = sb("xT", [P, KC, TOK])
        self.h_hi = sb("h_hi", [P, KC, TOK], F32R)
        self.h_lo = sb("h_lo", [P, KC, TOK], F32R)
        self.raw = sb("w_raw", [P, RAW, D])
        self.w_hi = sb("w_hi", [P, SPLIT, D], F32R)
        self.w_lo = sb("w_lo", [P, SPLIT, D], F32R)
        self.ident = sb("ident", [P, P])
        self.ones = sb("ones", [P, P])
        self.iota = sb("iota", [P, P])
        self.eps = sb("eps", [P, 1])
        self.mod = sb("mod", [P, 2, 2, 48])
        self.gs = sb("gs", [P, 2, 2, 2, KC])
        self.gains = sb("gains", [P, 6, KC])
        self.lb = sb("lb", [P, 2, 2, KC])
        self.psum = ctx.enter_context(nc.psum_tensor("psum", [P, 8, 512], F32))
        self.raw_in = [sem(f"raw_in{i}") for i in range(RAW)]
        self.raw_at = [0] * RAW
        self.hi_done = sem("w_hi_done")
        self.lo_done = sem("w_lo_done")
        self.tile_done = sem("tile_product_done")
        self.acc_free = [sem(f"acc_free{x}") for x in range(2)]
        self.settled = sem("settled")
        self.tiles = 0

    def sem(self, name):
        self.own.append(self.own_ctx.enter_context(self.nc.semaphore(name)))
        return self.own[-1]

    def retire(self):
        with self.nc.Block() as block:

            @block.gpsimd
            def _(pool):
                for s in self.own:
                    pool.sem_clear(s)
        self.own = []
        self.own_ctx.close()

    def settle(self, eng):
        eng.sem_inc(self.settled, 1)

    def load(self, sp, src, i, slot, n_raw, turn):
        sp.wait_ge(self.lo_done, i + (self.tiles + RAW - n_raw + 1))
        sp.dma_start(self.raw[:, slot, :], src).then_inc(self.raw_in[slot], 16)

    def hi(self, act, i, slot, s, turn):
        act.wait_ge(self.raw_in[slot], turn * 16 + (self.raw_at[slot] + 16))
        act.wait_ge(self.tile_done, i + (self.tiles + 1))
        act.activation(self.w_hi[:, s, :], self.raw[:, slot, :], ACT.Copy).then_inc(self.hi_done, 1)

    def lo(self, pool, i, slot, s):
        pool.wait_ge(self.hi_done, i + (self.tiles + 1))
        pool.tensor_tensor(self.w_lo[:, s, :], self.raw[:, slot, :], self.w_hi[:, s, :].bitcast(F32),
                           ALU.subtract).then_inc(self.lo_done, 1)

    def product(self, pe, i, s, tokens, hi, lo, ks=range(KC)):
        if ks[0] == 0:
            pe.wait_ge(self.lo_done, i + (self.tiles + RAW + 1))
            pe.wait_ge(self.acc_free[s], i // 2 + (self.tiles // 2 + 1))
        for k in ks:
            wh = self.w_hi[:, s, k * P:(k + 1) * P]
            wl = self.w_lo[:, s, k * P:(k + 1) * P]
            for n, (t0, w) in enumerate(halves(tokens)):
                out = self.psum[:, 2 * s + n, 0:w]
                pe.matmul(out, wh, hi[:, k, t0:t0 + w], start=(k == 0), stop=False)
                pe.matmul(out, wh, lo[:, k, t0:t0 + w], start=False, stop=False)
                last = pe.matmul(out, wl, hi[:, k, t0:t0 + w], start=False, stop=(k == KC - 1))
        if ks[-1] == KC - 1:
            last.then_inc(self.tile_done, 1)

    def wait_product(self, eng, i):
        eng.wait_ge(self.tile_done, i + (self.tiles + SPLIT + 1))

    def acc(self, s, tokens):
        hv = halves(tokens)
        return self.psum[:, 2 * s:2 * s + len(hv), 0:hv[0][1]]

    def end_stage(self, n, n_raw):
        self.tiles += n
        for s in range(n_raw):
            self.raw_at[s] += 16 * n // n_raw


def split_tokens(ap, tokens):
    return ap.rearrange("p (h w) -> p h w", h=len(halves(tokens)))


def norm_scales(t, dve, layer, done):
    for n in range(2):
        at = 24 * n + KC
        dve.scalar_tensor_tensor(out=t.gs[:, layer, n], in0=t.mod[:, layer, :, at:at + KC], scalar=1.0,
                                 in1=t.gains[:, 2 * n + layer].unsqueeze(1).to_broadcast([P, 2, KC]),
                                 op0=ALU.add, op1=ALU.mult).then_inc(done, 1)


def stage_setup(t):
    nc, a = t.nc, t.a
    with ExitStack() as ctx:
        sb = lambda n, s, d=F32: ctx.enter_context(nc.sbuf_tensor(n, s, d))
        cond = sb("cond", [P, KC, 2])
        scond = sb("scond", [P, KC, 2])
        bias = sb("ada_bias", [P, 2, 48])
        lbr = sb("lb_raw", [P, 2, 2, KC])
        lbm = sb("lb_max", [P, 2, KC])
        lbe = sb("lb_exp", [P, 2, 2, KC])
        lbs = sb("lb_sum", [P, 2, KC])
        row = sb("mod_row", [2, 6 * D])
        aw = sb("ada_w", [P, 3, KC, 512])
        small_in, x_in = t.sem("small_in"), t.sem("x_in")
        aw_in = [t.sem(f"ada_in{i}") for i in range(3)]
        const_done, id_zero = t.sem("const_done"), t.sem("id_zero")
        silu_done, row_mm, row_out = t.sem("silu_done"), t.sem("row_mm"), t.sem("row_out")
        flipped, mod_done, lb_step, lb_exp = t.sem("flipped"), t.sem("mod_done"), t.sem("lb_step"), t.sem("lb_exp")
        N = 6 * D // 512
        with nc.Block() as block:

            @block.sync
            def _(sp):
                sp.dma_start(cond[:], a["cond"]).then_inc(small_in, 16)
                sp.dma_start(t.gains[:], a["gains"]).then_inc(small_in, 16)
                sp.dma_start(bias[:], a["ada_b"]).then_inc(small_in, 16)
                sp.dma_start(lbr[:], a["hgrn_lb"]).then_inc(small_in, 16)
                with sp.Fori(0, N // 3) as q:
                    for s in range(3):
                        sp.wait_ge(row_mm, q * 3 + (s + 1))
                        sp.dma_start(aw[:, s], a["ada_w"][bass.ds(q * 3 + s, 1)].rearrange(
                            "a p k n -> p (a k) n")).then_inc(aw_in[s], 16)
                sp.dma_start(t.xT[:, :, 0:SEQ], a["x"]).then_inc(x_in, 16)
                sp.dma_start(t.xT[:, :, SEQ:TOK], a["ctx"]).then_inc(x_in, 16)
                sp.wait_ge(x_in, 32)

            @block.gpsimd
            def _(pool):
                pool.memset(t.ident[:], 0.0).then_inc(id_zero, 1)
                pool.memset(t.ones[:], 1.0).then_inc(const_done, 1)
                pool.memset(t.eps[:], EPS).then_inc(const_done, 1)
                pool.iota(t.iota[:], pattern=[[1, P]], base=0, channel_multiplier=0,
                          allow_small_or_imprecise_dtypes=True).then_inc(const_done, 1)
                pool.wait_ge(id_zero, 1)
                pool.affine_select(out=t.ident[:], in_=t.ident[:], compare_op=ALU.not_equal, fill=1.0,
                                   base=0, pattern=[[-1, P]], channel_multiplier=1).then_inc(const_done, 1)
                pool.wait_ge(const_done, 4)

            @block.scalar
            def _(act):
                act.wait_ge(small_in, 64)
                act.activation(scond[:], cond[:], ACT.Silu).then_inc(silu_done, 1)
                act.wait_ge(lb_step, 2)
                act.activation(lbe[:], lbr[:], ACT.Exp).then_inc(lb_exp, 1)
                with act.Fori(0, N // 2) as q:
                    for s in range(2):
                        act.wait_ge(row_mm, q * 2 + (3 + s + 1))
                        act.activation(row[:, bass.ds(q * 1024 + s * 512, 512)], t.psum[0:2, s, :],
                                       ACT.Copy).then_inc(row_out, 1)

            @block.tensor
            def _(pe):
                pe.sem_inc(row_mm, 3)
                pe.sem_inc(row_out, 2)
                pe.sem_inc(t.lo_done, RAW)
                pe.sem_inc(t.tile_done, SPLIT)
                for x in range(2):
                    pe.sem_inc(t.acc_free[x], 1)
                pe.wait_ge(silu_done, 1)
                with pe.Fori(0, N // 6) as q:
                    for i in range(6):
                        pe.wait_ge(aw_in[i % 3], q * 32 + 16 * (i // 3 + 1))
                        pe.wait_ge(row_out, q * 6 + (i + 1))
                        for k in range(KC):
                            last = pe.matmul(t.psum[0:2, i % 2, :], scond[:, k, :], aw[:, i % 3, k, :],
                                             start=(k == 0), stop=(k == KC - 1))
                        last.then_inc(row_mm, 1)
                pe.wait_ge(row_out, N + 2)
                pe.wait_ge(const_done, 4)
                for j in range(48):
                    last = pe.transpose(t.psum[:, 2, 2 * j:2 * j + 2], row[:, j * P:(j + 1) * P], t.ident[0:2, 0:2])
                last.then_inc(flipped, 1)

            @block.vector
            def _(dve):
                dve.wait_ge(small_in, 64)
                dve.tensor_tensor(lbm[:], lbr[:, 0], lbr[:, 1], ALU.max).then_inc(lb_step, 1)
                dve.wait_ge(lb_step, 1)
                dve.tensor_tensor(lbr[:], lbr[:], lbm[:].unsqueeze(1).to_broadcast([P, 2, 2, KC]),
                                  ALU.subtract).then_inc(lb_step, 1)
                dve.wait_ge(lb_exp, 1)
                dve.tensor_tensor(lbs[:], lbe[:, 0], lbe[:, 1], ALU.add).then_inc(lb_step, 1)
                dve.wait_ge(lb_step, 3)
                dve.reciprocal(lbm[:], lbs[:]).then_inc(lb_step, 1)
                dve.wait_ge(lb_step, 4)
                dve.tensor_tensor(lbr[:], lbe[:], lbm[:].unsqueeze(1).to_broadcast([P, 2, 2, KC]),
                                  ALU.mult).then_inc(lb_step, 1)
                dve.wait_ge(lb_step, 5)
                dve.tensor_tensor(lbs[:], lbr[:, 0], lbr[:, 1], ALU.add).then_inc(lb_step, 1)
                dve.wait_ge(lb_step, 6)
                dve.tensor_tensor(t.lb[:, 0], lbs[:], lbr[:, 0], ALU.subtract).then_inc(lb_step, 1)
                dve.wait_ge(lb_step, 7)
                dve.tensor_scalar(t.lb[:, 1], t.lb[:, 0], -1.0, 1.0, ALU.mult, ALU.add).then_inc(lb_step, 1)
                dve.wait_ge(flipped, 1)
                dve.tensor_tensor(t.mod[:, 0], t.psum[:, 2, 0:96].rearrange("p (j c) -> p c j", c=2),
                                  bias[:, 0].unsqueeze(1).to_broadcast([P, 2, 48]), ALU.add).then_inc(mod_done, 1)
                dve.wait_ge(mod_done, 1)
                norm_scales(t, dve, 0, mod_done)
                dve.wait_ge(mod_done, 3)
                dve.wait_ge(lb_step, 8)


def stage_norm(t, layer, n, tokens):
    nc = t.nc
    final = n == 2
    tag = f"n{layer}{n}"
    hv = halves(tokens)
    segs = [(0, SEQ, 0)] + ([(SEQ, CTX, 1)] if tokens == TOK else [])
    with ExitStack() as ctx:
        sb = lambda nm, s, d=F32: ctx.enter_context(nc.sbuf_tensor(nm + tag, s, d))
        sq = sb("sq", [P, 2, tokens])
        rs = sb("rs", [P, tokens])
        rstd = sb("rstd", [P, tokens])
        xn = sb("xn", [P, 3, tokens])
        out = sb("out", [P, KC, tokens]) if final else None
        sq_done = [t.sem(f"sq{s}{tag}") for s in ("_act", "_dve")]
        sum_part, root, rstd_done = (t.sem(s + tag) for s in ("sums", "root", "rstd"))
        xn_done, hi_done, lo_done = (t.sem(s + tag) for s in ("xn_", "hi_", "lo_"))
        stored = t.sem("stored" + tag) if final else None
        shift = lambda k, c: t.mod[:, layer, c, 24 * n + k:24 * n + k + 1]
        with nc.Block() as block:

            @block.scalar
            def _(act):
                for k in range(0, KC, 2):
                    if k >= 2:
                        act.wait_ge(sum_part, k - 1)
                    act.activation(sq[:, 0], t.xT[:, k, 0:tokens], ACT.Square).then_inc(sq_done[0], 1)
                act.wait_ge(sum_part, KC)
                act.activation(split_tokens(rs[:], tokens), t.acc(0, tokens), ACT.Sqrt, bias=t.eps[:],
                               scale=1.0 / D).then_inc(root, 1)
                if final:
                    return
                for k in range(KC):
                    act.wait_ge(xn_done, len(segs) * (k + 1))
                    for t0, w, c in segs:
                        act.activation(t.h_hi[:, k, t0:t0 + w], xn[:, k % 3, t0:t0 + w], ACT.Identity,
                                       bias=shift(k, c)).then_inc(hi_done, 1)

            @block.tensor
            def _(pe):
                for k in range(KC):
                    pe.wait_ge(sq_done[k % 2], k // 2 + 1)
                    for i, (t0, w) in enumerate(hv):
                        last = pe.matmul(t.psum[:, i, 0:w], t.ones[:], sq[:, k % 2, t0:t0 + w],
                                         start=(k == 0), stop=(k == KC - 1))
                    last.then_inc(sum_part, 1)

            @block.vector
            def _(dve):
                for k in range(1, KC, 2):
                    if k >= 2:
                        dve.wait_ge(sum_part, k - 1)
                    x = t.xT[:, k, 0:tokens]
                    dve.tensor_tensor(sq[:, 1], x, x, ALU.mult).then_inc(sq_done[1], 1)
                dve.wait_ge(root, 1)
                dve.reciprocal(rstd[:], rs[:]).then_inc(rstd_done, 1)
                dve.wait_ge(rstd_done, 1)
                if final:
                    for k in range(KC):
                        dve.scalar_tensor_tensor(out=out[:, k], in0=t.xT[:, k, 0:tokens],
                                                 scalar=t.gains[:, 4, k:k + 1], in1=rstd[:], op0=ALU.mult,
                                                 op1=ALU.mult).then_inc(xn_done, 1)
                    return

                def scaled(k):
                    if k >= 3:
                        dve.wait_ge(lo_done, len(segs) * (k - 2))
                    for t0, w, c in segs:
                        dve.scalar_tensor_tensor(out=xn[:, k % 3, t0:t0 + w], in0=t.xT[:, k, t0:t0 + w],
                                                 scalar=t.gs[:, layer, n, c, k:k + 1], in1=rstd[:, t0:t0 + w],
                                                 op0=ALU.mult, op1=ALU.mult).then_inc(xn_done, 1)
                for k in range(2):
                    scaled(k)
                for k in range(KC):
                    if k + 2 < KC:
                        scaled(k + 2)
                    dve.wait_ge(hi_done, len(segs) * (k + 1))
                    for t0, w, c in segs:
                        dve.scalar_tensor_tensor(out=t.h_lo[:, k, t0:t0 + w], in0=xn[:, k % 3, t0:t0 + w],
                                                 scalar=shift(k, c), in1=t.h_hi[:, k, t0:t0 + w].bitcast(F32),
                                                 op0=ALU.add, op1=ALU.subtract).then_inc(lo_done, 1)
                dve.wait_ge(lo_done, len(segs) * KC)

            @block.sync
            def _(sp):
                if final:
                    for k in range(KC):
                        sp.wait_ge(xn_done, k + 1)
                        sp.dma_start(t.a["out"][:, k], out[:, k]).then_inc(stored, 16)
                    sp.wait_ge(stored, 16 * KC)


def conv_rows():
    return [(0, SEQ // GRID_W, GRID_W), (SEQ, 1, CTX)]


def stage_conv(t, y_hi, y_lo):
    nc = t.nc
    T = TOK
    n = 3 * KC
    BODY = 12
    ADA_SLOTS = 6
    ADA = 48 * BODY // n
    with ExitStack() as ctx:
        sb = lambda nm, s, d=F32: ctx.enter_context(nc.sbuf_tensor(nm, s, d))
        kern = sb("kern", [P, KC, 3])
        gc = sb("gate_c", [P, T])
        z = sb("z", [P, T])
        zc = sb("zc", [P, T])
        y = sb("y", [P, T])
        cond = sb("cond_rows", [P, 2, D])
        aw = sb("ada_rows", [P, ADA_SLOTS, D])
        product = sb("ada_product", [P, D])
        dots = sb("ada_dots", [P, 2, ADA])
        bias = sb("ada_bias1", [P, 2, 48])
        cond_in, cond_done, ada_done, mod_done = (t.sem("ada1_" + x) for x in ("cond_in", "cond", "dots", "mod"))
        ada_in = [t.sem(f"ada1_in{x}") for x in range(ADA_SLOTS)]
        k_in = t.sem("kern_in")
        gc_done, z_done, conv_step = t.sem("gc_done"), t.sem("z_done"), t.sem("conv_step")
        y_done, yhi_done, ylo_done = t.sem("y_done"), t.sem("yhi_done"), t.sem("ylo_done")
        STEPS = 5
        with nc.Block() as block:

            @block.sync
            def _(sp):
                sp.dma_start(kern[:], t.a["conv_k"]).then_inc(k_in, 16)
                sp.dma_start(cond[:], t.a["cond_rows"]).then_inc(cond_in, 16)
                sp.dma_start(bias[:], t.a["ada_b"]).then_inc(k_in, 16)
                with sp.Fori(0, n // BODY) as q:
                    for i in range(BODY):
                        t.load(sp, t.a["conv_w_in"][bass.ds(q * BODY + i, 1)].rearrange("a p n -> p (a n)"),
                               q * BODY + i, i % RAW, RAW, None)
                        for j in range(2 * i, 2 * i + 2):
                            sp.wait_ge(ada_done, q * (2 * ADA) + (2 * j + 3))
                            sp.dma_start(aw[:, j % ADA_SLOTS], t.a["ada_w1"][bass.ds(q * ADA + j, 1)].rearrange(
                                "a p n -> p (a n)")).then_inc(ada_in[j % ADA_SLOTS], 16)

            @block.gpsimd
            def _(pool):
                with pool.Fori(0, n // BODY) as q:
                    for i in range(BODY):
                        t.lo(pool, q * BODY + i, i % RAW, i % SPLIT)

            @block.tensor
            def _(pe):
                with pe.Fori(0, n // BODY) as q:
                    for i in range(BODY):
                        t.product(pe, q * BODY + i, i % SPLIT, T, t.h_hi, t.h_lo)

            @block.scalar
            def _(act):
                def evac(q, i):
                    m = i // 3
                    c = q * (BODY // 3) + m
                    if i % 3 == 0:
                        t.wait_product(act, q * BODY + i)
                        act.wait_ge(z_done, c + 1)
                        act.activation(split_tokens(gc[:], T), t.acc(i % SPLIT, T), ACT.Copy).then_inc(gc_done, 1)
                        act.wait_ge(gc_done, c + 1)
                        act.sem_inc(t.acc_free[i % SPLIT], 1)
                    if i % 3 == 2:
                        act.wait_ge(y_done, c + 1)
                        act.activation(y_hi[:, bass.ds(c, 1), :].rearrange("p a n -> p (a n)"), y[:],
                                       ACT.Copy).then_inc(yhi_done, 1)
                act.wait_ge(cond_in, 16)
                act.activation(cond[:], cond[:], ACT.Silu).then_inc(cond_done, 1)
                with act.Fori(0, n // BODY) as q:
                    for i in range(BODY):
                        t.hi(act, q * BODY + i, i % RAW, i % SPLIT, q * (BODY // RAW) + i // RAW)
                        if i >= 1:
                            evac(q, i - 1)
                    evac(q, BODY - 1)

            @block.vector
            def _(dve):
                dve.sem_inc(z_done, 1)
                dve.sem_inc(ylo_done, 1)
                dve.wait_ge(k_in, 32)
                dve.wait_ge(cond_done, 1)
                dve.sem_inc(ada_done, 2 * ADA_SLOTS + 1)

                def ada(q, j):
                    dve.wait_ge(ada_in[j % ADA_SLOTS], q * (16 * ADA // ADA_SLOTS) + 16 * (j // ADA_SLOTS + 1))
                    dve.wait_ge(ada_done, q * (2 * ADA) + (2 * j + 2 * ADA_SLOTS + 1))
                    t.settle(dve)
                    row = aw[:, j % ADA_SLOTS]
                    for c in range(2):
                        dve.tensor_tensor_reduce(row if c else product[:], row, cond[:, c], 1.0, 0.0, ALU.mult,
                                                 ALU.add, dots[:, c, j:j + 1]).then_inc(ada_done, 1)
                with dve.Fori(0, n // BODY) as q:
                    for m in range(BODY // 3):
                        c = q * (BODY // 3) + m
                        i = 3 * m
                        t.wait_product(dve, q * BODY + (i + 1))
                        dve.wait_ge(gc_done, c + 1)
                        dve.tensor_tensor(split_tokens(z[:], T), split_tokens(gc[:], T),
                                          t.acc((i + 1) % SPLIT, T), ALU.mult).then_inc(z_done, 1)
                        dve.wait_ge(z_done, c + 2)
                        dve.sem_inc(t.acc_free[(i + 1) % SPLIT], 1)
                        for j in range(6 * m, 6 * m + 3):
                            ada(q, j)
                        kk = kern[:, bass.ds(c, 1), :].rearrange("p a n -> p (a n)")
                        dve.tensor_scalar(zc[:], z[:], kk[:, 1:2], None, ALU.mult).then_inc(conv_step, 1)
                        s = 1
                        for tap in (0, 2):
                            dve.wait_ge(conv_step, c * STEPS + s)
                            for t0, rows, w in conv_rows():
                                zr = z[:, t0:t0 + rows * w].rearrange("p (r w) -> p r w", w=w)
                                cr = zc[:, t0:t0 + rows * w].rearrange("p (r w) -> p r w", w=w)
                                src = zr[:, :, 0:w - 1] if tap == 0 else zr[:, :, 1:w]
                                dst = cr[:, :, 1:w] if tap == 0 else cr[:, :, 0:w - 1]
                                dve.scalar_tensor_tensor(out=dst, in0=src, scalar=kk[:, tap:tap + 1], in1=dst,
                                                         op0=ALU.mult, op1=ALU.add).then_inc(conv_step, 1)
                                s += 1
                        t.wait_product(dve, q * BODY + (i + 2))
                        dve.wait_ge(conv_step, c * STEPS + STEPS)
                        dve.wait_ge(ylo_done, c + 1)
                        dve.tensor_tensor(split_tokens(y[:], T), split_tokens(zc[:], T),
                                          t.acc((i + 2) % SPLIT, T), ALU.mult).then_inc(y_done, 1)
                        dve.wait_ge(y_done, c + 1)
                        dve.sem_inc(t.acc_free[(i + 2) % SPLIT], 1)
                        dve.wait_ge(yhi_done, c + 1)
                        dve.tensor_tensor(y_lo[:, bass.ds(c, 1), :].rearrange("p a n -> p (a n)"), y[:],
                                          y_hi[:, bass.ds(c, 1), :].rearrange("p a n -> p (a n)").bitcast(F32),
                                          ALU.subtract).then_inc(ylo_done, 1)
                        for j in range(6 * m + 3, 6 * m + 6):
                            ada(q, j)
                    dve.wait_ge(ada_done, q * (2 * ADA) + (2 * ADA + 2 * ADA_SLOTS + 1))
                    dve.tensor_tensor(t.mod[:, 1, :, bass.ds(q * ADA, ADA)], dots[:],
                                      bias[:, 1, bass.ds(q * ADA, ADA)].unsqueeze(1).to_broadcast([P, 2, ADA]),
                                      ALU.add).then_inc(mod_done, 1)
                dve.wait_ge(mod_done, n // BODY)
                norm_scales(t, dve, 1, mod_done)
                dve.wait_ge(mod_done, n // BODY + 2)
                dve.wait_ge(ylo_done, KC + 1)
        t.end_stage(n, RAW)


def stage_mix_out(t, layer, w_name, tokens, y_hi, y_lo):
    nc = t.nc
    segs = [(0, SEQ, 0)] + ([(SEQ, CTX, 1)] if tokens == TOK else [])
    with ExitStack() as ctx:
        tmp = ctx.enter_context(nc.sbuf_tensor(f"mix{layer}", [P, 2, tokens], F32))
        copied, added = t.sem(f"mix_copied{layer}"), t.sem(f"mix_added{layer}")
        with nc.Block() as block:

            @block.sync
            def _(sp):
                for i in range(KC):
                    t.load(sp, t.a[w_name][i], i, i % RAW, RAW, None)

            @block.gpsimd
            def _(pool):
                for i in range(KC):
                    t.lo(pool, i, i % RAW, i % SPLIT)

            @block.tensor
            def _(pe):
                for i in range(KC):
                    t.product(pe, i, i % SPLIT, tokens, y_hi, y_lo)

            @block.scalar
            def _(act):
                def evac(i):
                    t.wait_product(act, i)
                    if i >= 2:
                        act.wait_ge(added, len(segs) * (i - 1))
                    act.activation(split_tokens(tmp[:, i % 2], tokens), t.acc(i % SPLIT, tokens),
                                   ACT.Copy).then_inc(copied, 1)
                    act.wait_ge(copied, i + 1)
                    act.sem_inc(t.acc_free[i % SPLIT], 1)
                for i in range(KC):
                    t.hi(act, i, i % RAW, i % SPLIT, i // RAW)
                    if i >= 1:
                        evac(i - 1)
                evac(KC - 1)

            @block.vector
            def _(dve):
                for i in range(KC):
                    dve.wait_ge(copied, i + 1)
                    for t0, w, c in segs:
                        dve.scalar_tensor_tensor(out=t.xT[:, i, t0:t0 + w], in0=tmp[:, i % 2, t0:t0 + w],
                                                 scalar=t.mod[:, layer, c, 16 + i:17 + i],
                                                 in1=t.xT[:, i, t0:t0 + w], op0=ALU.mult,
                                                 op1=ALU.add).then_inc(added, 1)
                dve.wait_ge(added, len(segs) * KC)
        t.end_stage(KC, RAW)


def stage_rank(t, layer, tokens, top, top_i):
    nc = t.nc
    blocks = tokens // P
    n, BODY = LISTS, 4
    tag = f"r{layer}"
    with ExitStack() as ctx:
        sb = lambda nm, s, d=F32: ctx.enter_context(nc.sbuf_tensor(nm + tag, s, d))
        keys = sb("keys", [P, LISTS, NKEYS])
        qT = sb("qT", [P, 2, tokens])
        sc = sb("sc", [P, 2, blocks, NKEYS])
        t8 = sb("t8", [P, 2, blocks, 2, 8])
        i8 = sb("i8", [P, 2, blocks, 2, 8], U32)
        k_in, q_done, s_mm, s_done = (t.sem(x + tag) for x in ("keys_in", "q_done", "s_mm", "s_done"))
        rank, taken, taken_v, s_cp = (t.sem(x + tag) for x in ("rank", "taken", "taken_v", "s_cp"))

        def score_bank(b):
            return t.psum[:, 4 + b // 4, (b % 4) * P:(b % 4 + 1) * P]

        with nc.Block() as block:

            @block.sync
            def _(sp):
                sp.dma_start(keys[:], t.a["peer_keys"][layer]).then_inc(k_in, 16)
                with sp.Fori(0, n // BODY) as q:
                    for i in range(BODY):
                        t.load(sp, t.a[f"peer_w_q{layer}"][bass.ds(q * BODY + i, 1)].rearrange(
                            "a p n -> p (a n)"), q * BODY + i, i % RAW, RAW, None)

            @block.gpsimd
            def _(pool):
                with pool.Fori(0, n // BODY) as q:
                    for i in range(BODY):
                        t.lo(pool, q * BODY + i, i % RAW, i % SPLIT)

            @block.tensor
            def _(pe):
                pe.wait_ge(k_in, 16)

                def scores(c, i):
                    pe.wait_ge(q_done, c + 1)
                    pe.wait_ge(s_done, c + 1)
                    for b in range(blocks):
                        last = pe.matmul(score_bank(b), qT[:, i % 2, b * P:(b + 1) * P],
                                         keys[:, bass.ds(c, 1), :].rearrange("p a n -> p (a n)"),
                                         start=True, stop=True)
                    last.then_inc(s_mm, 1)
                t.product(pe, 0, 0, tokens, t.h_hi, t.h_lo)
                with pe.Fori(0, n // BODY - 1) as q:
                    for i in range(BODY):
                        t.product(pe, q * BODY + (i + 1), (i + 1) % SPLIT, tokens, t.h_hi, t.h_lo)
                        scores(q * BODY + i, i)
                for i in range(n - BODY, n):
                    if i + 1 < n:
                        t.product(pe, i + 1, (i + 1) % SPLIT, tokens, t.h_hi, t.h_lo)
                    scores(i, i)

            @block.scalar
            def _(act):
                act.sem_inc(s_done, 1)
                act.sem_inc(taken, 2)

                def query(c, i):
                    t.wait_product(act, c)
                    act.wait_ge(s_mm, c + 1)
                    act.activation(split_tokens(qT[:, i % 2], tokens), t.acc(i % SPLIT, tokens),
                                   ACT.Copy).then_inc(q_done, 1)
                    act.wait_ge(q_done, c + 1)
                    act.sem_inc(t.acc_free[i % SPLIT], 1)

                def score(c, i):
                    act.wait_ge(s_mm, c + 3)
                    act.wait_ge(taken, c + 1)
                    for h in range(0, blocks, 4):
                        m = min(4, blocks - h)
                        last = act.activation(sc[:, i % 2, h:h + m], t.psum[:, 4 + h // 4, 0:m * P].rearrange(
                            "p (b k) -> p b k", k=P), ACT.Copy)
                        last.then_inc(s_cp, 1)
                    act.wait_ge(s_cp, (c + 1) * ((blocks + 3) // 4))
                    act.sem_inc(s_done, 1)
                act.sem_inc(s_mm, 2)
                for i in range(SPLIT):
                    t.hi(act, i, i % RAW, i % SPLIT, 0)
                with act.Fori(0, n // BODY - 1) as q:
                    for i in range(BODY):
                        c = q * BODY + i
                        query(c, i)
                        t.hi(act, c + SPLIT, (i + SPLIT) % RAW, i % SPLIT, q + (i + SPLIT) // RAW)
                        score(c, i)
                for i in range(n - BODY, n):
                    query(i, i)
                    if i + SPLIT < n:
                        t.hi(act, i + SPLIT, (i + SPLIT) % RAW, i % SPLIT, (i + SPLIT) // RAW)
                    score(i, i)

            @block.vector
            def _(dve):
                with dve.Fori(0, n // BODY) as q:
                    for i in range(BODY):
                        c = q * BODY + i
                        s = i % 2
                        dve.wait_ge(s_done, c + 2)
                        t.settle(dve)
                        for b in range(blocks):
                            dve.max(t8[:, s, b, 0], sc[:, s, b]).then_inc(rank, 1)
                        dve.wait_ge(rank, c * (5 * blocks) + blocks)
                        t.settle(dve)
                        for b in range(blocks):
                            dve.max_index(i8[:, s, b, 0], t8[:, s, b, 0], sc[:, s, b]).then_inc(rank, 1)
                        dve.wait_ge(rank, c * (5 * blocks) + 2 * blocks)
                        t.settle(dve)
                        for b in range(blocks):
                            dve.match_replace(sc[:, s, b], t8[:, s, b, 0], sc[:, s, b], LOWEST).then_inc(rank, 1)
                        dve.wait_ge(rank, c * (5 * blocks) + 3 * blocks)
                        t.settle(dve)
                        for b in range(blocks):
                            dve.max(t8[:, s, b, 1], sc[:, s, b]).then_inc(rank, 1)
                        dve.wait_ge(rank, c * (5 * blocks) + 4 * blocks)
                        t.settle(dve)
                        for b in range(blocks):
                            dve.max_index(i8[:, s, b, 1], t8[:, s, b, 1], sc[:, s, b]).then_inc(rank, 1)
                        dve.wait_ge(rank, c * (5 * blocks) + 5 * blocks)
                        dst = lambda x: x[:, :, bass.ds(c, 1), :].rearrange("p b a k -> p b (a k)")
                        dve.tensor_copy(dst(top), t8[:, s].rearrange("p b a k -> p b (a k)")).then_inc(taken_v, 1)
                        dve.tensor_copy(dst(top_i), i8[:, s].rearrange("p b a k -> p b (a k)")).then_inc(taken_v, 1)
                        dve.wait_ge(taken_v, c * 2 + 2)
                        dve.sem_inc(taken, 1)
        t.end_stage(n, RAW)


def stage_gates(t, layer, tokens, top, top_i, g_dram, act_dram):
    nc = t.nc
    A = AHEAD[layer]
    blocks = tokens // P
    tag = f"g{layer}"
    K = TOPK
    STAGES, STEPS_S = P // STAGE_T, STAGE_T // 8
    PRE = A - STAGES
    with ExitStack() as ctx:
        sb = lambda nm, s, d=F32: ctx.enter_context(nc.sbuf_tensor(nm + tag, s, d))
        cand = sb("cand", [P, HEADS, K, K])
        pick = sb("pick", [P, HEADS, K, K])
        best = sb("best", [P, HEADS, K])
        pos = sb("pos", [P, HEADS, K], U32)
        half_u = sb("half_u", [P, 2, HEADS * K], U32)
        half = sb("half", [P, 2, HEADS * K])
        topf = sb("topf", [P, LISTS, K])
        sel = sb("sel", [P, 3, HEADS * K])
        ex = sb("ex", [P, HEADS, K])
        den = sb("den", [P, HEADS])
        selT = sb("selT", [P, 3, P])
        oi = sb("oi", [P, 8, P])
        oj = sb("oj", [P, 8, P])
        stage = sb("stage", [P, 2, NKEYS, STAGE_T])
        act_f = sb("act_g", [P, 2, tokens])
        gelu_done = t.sem("gelu_done" + tag)
        spilled = [t.sem(f"spilled{x}{tag}") for x in range(2)]
        dv, ex_in, ex_done = (t.sem(x + tag) for x in ("dv", "ex_in", "ex_done"))
        sel_T, selT_cp, oh_ready, g_mm, g_cp = (t.sem(x + tag) for x in ("sel_T", "selT_cp", "oh_ready", "g_mm", "g_cp"))
        stored = [t.sem(f"stored{x}{tag}") for x in range(2)]
        DV = 1 + 5 + 2 + 1 + 2 * 3 + 3 + 1
        with nc.Block() as block:

            @block.vector
            def _(dve):
                dve.sem_inc(g_mm, 2)
                dve.sem_inc(selT_cp, 1)
                bc = lambda ap, shape: ap.to_broadcast(shape)
                with dve.Fori(0, blocks) as b:
                    n = [0]

                    def step(ins):
                        n[0] += 1
                        ins.then_inc(dv, 1)
                        dve.wait_ge(dv, b * DV + n[0])
                    tb = top[:, bass.ds(b, 1), :, :].rearrange("p a (h c) k -> p (a h) c k", c=2)
                    step(dve.tensor_tensor(cand[:], bc(tb[:, :, 0, :].unsqueeze(3), [P, HEADS, K, K]),
                                           bc(tb[:, :, 1, :].unsqueeze(2), [P, HEADS, K, K]), ALU.add))
                    flat = lambda h: cand[:, h].rearrange("p a b -> p (a b)")
                    for part in range(2):
                        o = 8 * part
                        t.settle(dve)
                        for h in range(HEADS):
                            last = dve.max(best[:, h, o:o + 8], flat(h))
                        step(last)
                        t.settle(dve)
                        for h in range(HEADS):
                            last = dve.max_index(pos[:, h, o:o + 8], best[:, h, o:o + 8], flat(h))
                        step(last)
                        if part == 0:
                            t.settle(dve)
                            for h in range(HEADS):
                                last = dve.match_replace(flat(h), best[:, h, 0:8], flat(h), LOWEST)
                            step(last)
                    pf = pos[:].rearrange("p h k -> p (h k)")
                    dve.tensor_single_scalar(half_u[:, 0], pf, 4, ALU.logical_shift_right)
                    step(dve.tensor_single_scalar(half_u[:, 1], pf, 15, ALU.bitwise_and))
                    dve.tensor_copy(topf[:], top_i[:, bass.ds(b, 1), :, :].rearrange("p a l k -> p (a l) k"))
                    step(dve.tensor_copy(half[:], half_u[:]))
                    step(dve.tensor_tensor(ex[:], best[:], bc(best[:, :, 0:1], [P, HEADS, K]), ALU.subtract))
                    dve.sem_inc(ex_in, 1)
                    tf = topf[:].rearrange("p (h c) k -> p h c k", c=2)
                    for c in range(2):
                        step(dve.tensor_tensor(
                            pick[:], bc(half[:, c].rearrange("p (h k) -> p h k", k=K).unsqueeze(3), [P, HEADS, K, K]),
                            bc(t.iota[:, 0:K].unsqueeze(1).unsqueeze(1), [P, HEADS, K, K]), ALU.is_equal))
                        step(dve.tensor_tensor(pick[:], pick[:], bc(tf[:, :, c, :].unsqueeze(2), [P, HEADS, K, K]),
                                               ALU.mult))
                        step(dve.tensor_reduce(sel[:, c].rearrange("p (h k) -> p h k", k=K), pick[:], AX.X, ALU.add))
                    dve.wait_ge(ex_done, b + 1)
                    step(dve.tensor_reduce(den[:], ex[:], AX.X, ALU.add))
                    step(dve.reciprocal(den[:], den[:]))
                    step(dve.tensor_tensor(sel[:, 2].rearrange("p (h k) -> p h k", k=K), ex[:],
                                           bc(den[:].unsqueeze(2), [P, HEADS, K]), ALU.mult))
                    dve.wait_ge(sel_T, b + 1)
                    dve.wait_ge(g_mm, b * (P // 4) + 2)
                    step(dve.tensor_copy(selT[:], t.psum[:, 6, 0:3 * P].rearrange("p (c x) -> p c x", x=P)))
                    dve.sem_inc(selT_cp, 1)
                    for q in range(P // 8):
                        for u in range(2):
                            dve.wait_ge(g_mm, b * (P // 4) + q * 2 + (u + 1))
                            for r in range(4 * u, 4 * u + 4):
                                col = lambda c: selT[:, c, q * 8 + r:q * 8 + r + 1]
                                dve.tensor_scalar(oi[:, r], t.iota[:], col(0), None, ALU.is_equal)
                                last = dve.tensor_scalar(oj[:, r], t.iota[:], col(1), col(2), ALU.is_equal, ALU.mult)
                            last.then_inc(oh_ready, 1)
                assert n[0] == DV, n

            @block.tensor
            def _(pe):
                pe.sem_inc(g_cp, 2)
                up = lambda c, i, ks=range(KC): t.product(pe, c, i % SPLIT, tokens, t.h_hi, t.h_lo, ks)
                with pe.Fori(0, blocks) as b:
                    for i in range(PRE):
                        up(b * A + i, i)
                    pe.wait_ge(dv, b * DV + (DV - 1))
                    pe.wait_ge(selT_cp, b + 1)
                    for c in range(3):
                        last = pe.transpose(t.psum[:, 6, c * P:(c + 1) * P], sel[:, c], t.ident[:])
                    last.then_inc(sel_T, 1)
                    for i in range(PRE, A):
                        for k in range(KC):
                            u, g = k % 2, (i - PRE) * KC + k
                            pe.wait_ge(oh_ready, b * (P // 4) + (g + 1))
                            pe.wait_ge(g_cp, b * (P // 4) + (g + 1))
                            for r in range(4):
                                last = pe.matmul(t.psum[:, 4 + u, r * P:(r + 1) * P], oi[:, 4 * u + r],
                                                 oj[:, 4 * u + r], start=True, stop=True)
                            last.then_inc(g_mm, 1)
                            up(b * A + i, i, [k])

            @block.scalar
            def _(act):
                for x in range(2):
                    act.sem_inc(stored[x], 16)

                def ahead(b, i):
                    c = b * A + i
                    t.wait_product(act, c)
                    act.wait_ge(spilled[i % 2], b * (16 * A // 2) + 16 * (i // 2 + 1))
                    act.activation(split_tokens(act_f[:, i % 2], tokens), t.acc(i % SPLIT, tokens),
                                   ACT.Gelu).then_inc(gelu_done, 1)
                    act.wait_ge(gelu_done, c + 1)
                    act.sem_inc(t.acc_free[i % SPLIT], 1)
                    t.hi(act, c + SPLIT, (i + SPLIT) % RAW, i % SPLIT, b * (A // RAW) + (i + SPLIT) // RAW)
                for x in range(2):
                    act.sem_inc(spilled[x], 16)
                for i in range(SPLIT):
                    t.hi(act, i, i, i, 0)
                with act.Fori(0, blocks) as b:
                    for i in range(PRE):
                        ahead(b, i)
                        if i == 3 * PRE // 4 - 1:
                            act.wait_ge(ex_in, b + 1)
                            act.activation(ex[:], ex[:], ACT.Exp).then_inc(ex_done, 1)
                    for s in range(STAGES):
                        act.wait_ge(stored[s % 2], b * (16 * STAGES // 2) + 16 * (s // 2 + 1))
                        with act.Fori(0, STEPS_S) as q:
                            for u in range(2):
                                act.wait_ge(g_mm, b * (P // 4) + q * 2 + (s * (STAGE_T // 4) + u + 3))
                                act.activation(stage[:, s % 2, :, bass.ds(q * 8 + 4 * u, 4)],
                                               t.psum[:, 4 + u, :].rearrange("p (t j) -> p j t", j=NKEYS),
                                               ACT.Copy).then_inc(g_cp, 1)
                        ahead(b, PRE + s)

            @block.gpsimd
            def _(pool):
                for i in range(SPLIT):
                    t.lo(pool, i, i, i)
                with pool.Fori(0, blocks) as b:
                    for i in range(A):
                        t.lo(pool, b * A + (i + SPLIT), (i + SPLIT) % RAW, i % SPLIT)

            @block.sync
            def _(sp):
                def load(c, i):
                    t.load(sp, t.a[f"peer_u{layer}"][bass.ds(c, 1)].rearrange("a p n -> p (a n)"),
                           c, i % RAW, RAW, None)

                def ahead(b, i):
                    sp.wait_ge(gelu_done, b * A + (i + 1))
                    sp.dma_start(act_dram[bass.ds(b * A + i, 1)].rearrange("a p x -> p (a x)"),
                                 act_f[:, i % 2]).then_inc(spilled[i % 2], 16)
                    load(b * A + (i + RAW), i)
                for i in range(RAW):
                    load(i, i)
                with sp.Fori(0, blocks) as b:
                    for i in range(PRE):
                        ahead(b, i)
                    for s in range(STAGES):
                        sp.wait_ge(g_cp, b * (P // 4) + ((s + 1) * (STAGE_T // 4) + 2))
                        sp.dma_start(
                            g_dram.rearrange("g i n x -> n i g x")[bass.ds(b * STAGES + s, 1)].rearrange(
                                "a i g x -> i (a g) x"),
                            stage[:, s % 2].rearrange("p (g j) t -> p g (j t)", j=QUAD)).then_inc(stored[s % 2], 16)
                        ahead(b, PRE + s)
                for x in range(2):
                    sp.wait_ge(spilled[x], 16 * (blocks * A // 2 + 1))
                    sp.wait_ge(stored[x], 16 * (blocks * STAGES // 2 + 1))


def stage_experts(t, layer, tokens, g_dram, act_dram):
    nc = t.nc
    T = tokens
    segs = [(0, SEQ, 0)] + ([(SEQ, CTX, 1)] if tokens == TOK else [])
    NT = KC * len(segs)
    tag = f"e{layer}"
    n = NKEYS
    R = AHEAD[layer] * tokens // P
    QR = R // QUAD
    with ExitStack() as ctx:
        sb = lambda nm, s, d=F32: ctx.enter_context(nc.sbuf_tensor(nm + tag, s, d))
        act_in = [t.sem(f"act_in{x}{tag}") for x in range(2)]
        gt = sb("gt", [P, 2, QUAD * T])
        act_f = sb("act_f", [P, 2, T])
        a_hi = sb("a_hi", [P, 4, T], F32R)
        a_lo = sb("a_lo", [P, 4, T], F32R)
        vr = sb("v_raw", [P, 2, D])
        v_hi = sb("v_hi", [P, 4, D], F32R)
        v_lo = sb("v_lo", [P, 4, D], F32R)
        g_in, gelu_done, gated, ahi_done, alo_done = (
            t.sem(x + tag) for x in ("g_in", "gelu_done", "gated", "ahi_done", "alo_done"))
        act_free = t.sem("act_free" + tag)
        v_in = [t.sem(f"v_in{x}{tag}") for x in range(2)]
        vhi_done, vlo_done, out_mm, out_free, pair_done = (
            t.sem(x + tag) for x in ("vhi_done", "vlo_done", "out_mm", "out_free", "pair_done"))
        with nc.Block() as block:

            @block.sync
            def _(sp):
                sp.sem_inc(g_in, 1)

                def u_load(c, i, turn):
                    t.load(sp, t.a[f"peer_u{layer}"][bass.ds(c, 1)].rearrange("a p n -> p (a n)"),
                           c, i, RAW, turn)

                def quad(q, stored, more):
                    sp.wait_ge(g_in, q * 16 + 1)
                    sp.wait_ge(gated, q * QUAD + 1)
                    sp.dma_start(gt[:, bass.ds(q % 2, 1), :].rearrange("p a x -> p (a x)"),
                                 g_dram[bass.ds(q, 1)].rearrange("a i n x -> i (a n x)")).then_inc(g_in, 16)
                    for i in range(QUAD):
                        c = q * QUAD + i
                        if stored:
                            sp.wait_ge(act_free, c + 1)
                            sp.dma_start(act_f[:, i % 2], act_dram[bass.ds(c, 1)].rearrange(
                                "a p x -> p (a x)")).then_inc(act_in[i % 2], 16)
                        elif more:
                            u_load(c + RAW, i, None)
                        sp.wait_ge(vlo_done, c + 1)
                        sp.dma_start(vr[:, i % 2, :], t.a[f"peer_v{layer}"][bass.ds(c, 1)].rearrange(
                            "a p n -> p (a n)")).then_inc(v_in[i % 2], 16)
                with sp.Fori(0, QR) as q:
                    quad(q, True, False)
                with sp.Fori(QR, n // QUAD - 1) as q:
                    quad(q, False, True)
                quad(n // QUAD - 1, False, False)

            @block.gpsimd
            def _(pool):
                pool.sem_inc(vlo_done, 2)

                def v_low(c, i):
                    pool.wait_ge(vhi_done, c + 1)
                    pool.tensor_tensor(v_lo[:, i], vr[:, i % 2], v_hi[:, i].bitcast(F32),
                                       ALU.subtract).then_inc(vlo_done, 1)
                with pool.Fori(0, QR) as q:
                    for i in range(QUAD):
                        v_low(q * QUAD + i, i)
                with pool.Fori(QR, n // QUAD - 1) as q:
                    for i in range(QUAD):
                        t.lo(pool, q * QUAD + (i + SPLIT), (i + SPLIT) % RAW, i % SPLIT)
                        v_low(q * QUAD + i, i)
                for i in range(QUAD):
                    if i + SPLIT < QUAD:
                        t.lo(pool, n - QUAD + i + SPLIT, i + SPLIT, i % SPLIT)
                    v_low(n - QUAD + i, i)

            @block.tensor
            def _(pe):
                def pair(p, odd):
                    pe.wait_ge(alo_done, p * 2 + 2)
                    pe.wait_ge(vlo_done, p * 2 + 4)
                    for m in range(NT):
                        d, (t0, w, _) = m // len(segs), segs[m % len(segs)]
                        pe.wait_ge(out_free, p * NT + (m + 1))
                        for j in range(2):
                            sl = 2 * odd + j
                            vh, vl = (v[:, sl, d * P:(d + 1) * P] for v in (v_hi, v_lo))
                            out = t.psum[:, 4 + m % 4, 0:w]
                            pe.matmul(out, vh, a_hi[:, sl, t0:t0 + w], start=(j == 0), stop=False)
                            pe.matmul(out, vh, a_lo[:, sl, t0:t0 + w], start=False, stop=False)
                            last = pe.matmul(out, vl, a_hi[:, sl, t0:t0 + w], start=False, stop=(j == 1))
                        last.then_inc(out_mm, 1)
                up = lambda c, s: t.product(pe, c, s, T, t.h_hi, t.h_lo)
                pe.sem_inc(out_free, 4)
                with pe.Fori(0, QR - 1) as q:
                    for m in range(2):
                        pair(q * 2 + m, m)
                pair(R // 2 - 2, 0)
                up(R, 0)
                up(R + 1, 1)
                pair(R // 2 - 1, 1)
                with pe.Fori(QR, n // QUAD - 1) as q:
                    for m in range(2):
                        up(q * QUAD + (2 * m + 2), 0)
                        up(q * QUAD + (2 * m + 3), 1)
                        pair(q * 2 + m, m)
                up(n - 2, 0)
                up(n - 1, 1)
                pair(n // 2 - 2, 0)
                pair(n // 2 - 1, 1)

            @block.scalar
            def _(act):
                def chunk(c, i, stored, turn):
                    if not stored:
                        t.wait_product(act, c)
                        act.wait_ge(act_free, c + 1)
                        act.activation(split_tokens(act_f[:, i % 2], T), t.acc(i % 2, T),
                                       ACT.Gelu).then_inc(gelu_done, 1)
                        act.wait_ge(gelu_done, c - (R - 1))
                        act.sem_inc(t.acc_free[i % SPLIT], 1)
                    if turn is not None:
                        t.hi(act, c + SPLIT, (i + SPLIT) % RAW, i % SPLIT, turn)
                    act.wait_ge(v_in[i % 2], vturn(c, i))
                    act.wait_ge(pair_done, turn_q * 2 + (i // 2 + 1))
                    act.activation(v_hi[:, i, :], vr[:, i % 2, :], ACT.Copy).then_inc(vhi_done, 1)
                    act.wait_ge(gated, c + 6)
                    act.activation(a_hi[:, i, :], act_f[:, i % 2], ACT.Copy).then_inc(ahi_done, 1)
                act.sem_inc(act_free, 2)
                act.sem_inc(pair_done, 2)
                vturn = lambda c, i: turn_q * 32 + 16 * (i // 2 + 1)
                with act.Fori(0, QR) as q:
                    turn_q = q
                    for i in range(QUAD):
                        chunk(q * QUAD + i, i, True, None)
                with act.Fori(QR, n // QUAD - 1) as q:
                    turn_q = q
                    for i in range(QUAD):
                        chunk(q * QUAD + i, i, False, q + (i + SPLIT) // RAW)
                turn_q = n // QUAD - 1
                for i in range(QUAD):
                    chunk(n - QUAD + i, i, False, turn_q if i + SPLIT < QUAD else None)

            @block.vector
            def _(dve):
                def chunk(q, i, stored):
                    c = q * QUAD + i
                    if stored:
                        dve.wait_ge(act_in[i % 2], q * 32 + 16 * (i // 2 + 1))
                    else:
                        dve.wait_ge(gelu_done, c - (R - 1))
                    if i == 0:
                        dve.wait_ge(g_in, q * 16 + 17)
                    g = gt[:, bass.ds(q % 2, 1), :].rearrange("p a (n j t) -> p j (a n) t", j=QUAD, t=STAGE_T)[:, i]
                    a = act_f[:, i % 2].rearrange("p (n t) -> p n t", t=STAGE_T)
                    dve.tensor_tensor(a, a, g, ALU.mult).then_inc(gated, 1)
                    dve.wait_ge(ahi_done, c + 1)
                    dve.tensor_tensor(a_lo[:, i], act_f[:, i % 2], a_hi[:, i].bitcast(F32), ALU.subtract).then_inc(alo_done, 1)
                    dve.wait_ge(alo_done, c + 1)
                    dve.sem_inc(act_free, 1)

                def gather(p, part=None):
                    for m in range(NT) if part is None else range(part * NT // 2, (part + 1) * NT // 2):
                        d, (t0, w, cond) = m // len(segs), segs[m % len(segs)]
                        dve.wait_ge(out_mm, p * NT + (m + 1))
                        x = t.xT[:, d, t0:t0 + w]
                        dve.scalar_tensor_tensor(out=x, in0=t.psum[:, 4 + m % 4, 0:w],
                                                 scalar=t.mod[:, layer, cond, 40 + d:41 + d], in1=x,
                                                 op0=ALU.mult, op1=ALU.add).then_inc(out_free, 1)
                    if part != 0:
                        dve.wait_ge(out_free, p * NT + (NT + 4))
                        dve.sem_inc(pair_done, 1)
                dve.sem_inc(gated, 5)
                for i in range(QUAD):
                    chunk(0, i, True)
                    if i >= 2:
                        gather(0, i - 2)
                with dve.Fori(1, QR) as q:
                    for i in range(QUAD):
                        chunk(q, i, True)
                        gather(q * 2 + (i // 2 - 1), i % 2)
                with dve.Fori(QR, n // QUAD) as q:
                    for i in range(QUAD):
                        if i % 2:
                            gather(q * 2 + (i // 2 - 1))
                        chunk(q, i, False)
                gather(n // 2 - 1)
        t.end_stage(n, RAW)


def stage_hgrn(t, y):
    nc = t.nc
    n, PER, BODY, N_RAW = 5 * HEADS, 5, 10, 2
    LAYER = 1
    MID = (CHUNK // 2, CHUNK - 1 - CHUNK // 2)
    LAST = (CHUNK - 1, 0)
    ORDER = ([XCH + c for c in range(CCH)] + list(range(XCH)),
             [XCH + CCH - 1 - c for c in range(CCH)] + [XCH - 1 - c for c in range(XCH)])
    KV = [(s, d) for s in range(NCH - 1) for d in range(2)]
    ROWS = P // CHUNK
    KVG = [KV[i:i + 2 * ROWS] for i in range(0, len(KV), 2 * ROWS)]
    BLOCK = [[ORDER[d][ROWS * x] // ROWS for x in range(NCH // ROWS)] for d in range(2)]
    BLK = TOK // P
    with ExitStack() as ctx:
        sb = lambda nm, s, d=F32: ctx.enter_context(nc.sbuf_tensor(nm, s, d))
        f = [sb(f"f{d}", [P, TOK]) for d in range(2)]
        kk = [sb(f"kk{d}", [P, TOK]) for d in range(2)]
        b = [sb(f"b{d}", [P, TOK]) for d in range(2)]
        e = [sb(f"e{d}", [P, TOK]) for d in range(2)]
        qm = [sb(f"qm{d}", [P, SEQ]) for d in range(2)]
        km = [sb(f"km{d}", [P, SEQ]) for d in range(2)]
        qd = [sb(f"qd{d}", [P, SEQ]) for d in range(2)]
        dc = [sb(f"dc{d}", [P, NCH]) for d in range(2)]
        reset = sb("reset", [P, TOK])
        vT, qs, zs = sb("vT", [P, TOK]), sb("qs", [P, SEQ]), sb("zs", [P, 2, SEQ])
        v_tok = sb("v_tok", [P, BLK, P])
        v_by_chunk = sb("v_by_chunk", [P, BLK, ROWS, P])
        kd_tok = [sb(f"kd_tok{d}", [P, BLK, P]) for d in range(2)]
        probs = [sb(f"probs{d}", [P, SEQ]) for d in range(2)]
        same = [sb(f"same{d}", [P, P]) for d in range(2)]
        state = [t.raw[:, N_RAW:RAW].rearrange("p a (c x) -> p (a c) x", x=P), sb("state1", [P, XCH, P])]
        names = ("reset_done", "mask_done", "f_in", "v_in", "q_in", "z_in", "f_done", "k_done", "ln_done", "b_done",
                 "d1", "d1_exp", "m_done", "d2", "d2_exp", "kd_done", "b_exp", "qd_done", "dc_done",
                 "tok_mm", "tok_cp", "score_mm", "prob_done", "kv_mm", "st_done", "kv_free", "o_mm", "o_cp",
                 "osq", "osum", "oroot", "orstd", "on", "y_done", "vc_zero", "vc_done")
        S = {x: t.sem("h_" + x) for x in names}

        def turns(eng, turn):
            with eng.Fori(0, HEADS // 2 - 1) as q:
                for u in range(2):
                    turn(q, u, 1)
            turn(HEADS // 2 - 1, 0, 2)
            turn(HEADS // 2 - 1, 1, 0)
        xv = lambda ap: ap[:, 0:SEQ].rearrange("p (c l) -> p c l", l=CHUNK)
        av = lambda ap: ap[:].rearrange("p (c l) -> p c l", l=CHUNK)
        o = e[0][:, 0:SEQ]
        osq = e[1][:, 0:SEQ]
        orn, ony = km[0][:], km[1][:]
        with nc.Block() as block:

            @block.sync
            def _(sp):
                with sp.Fori(0, n // BODY) as q:
                    for i in range(BODY):
                        t.load(sp, t.a["hgrn_w_in"][bass.ds(q * BODY + i, 1)].rearrange("a p n -> p (a n)"),
                               q * BODY + i, i % N_RAW, N_RAW, None)

            @block.gpsimd
            def _(pool):
                pool.memset(reset[:], 1.0).then_inc(S["reset_done"], 1)
                for d in range(2):
                    pool.memset(same[d][:], 1.0).then_inc(S["mask_done"], 1)
                    pool.memset(probs[d][:], 0.0).then_inc(S["reset_done"], 1)
                pool.wait_ge(S["reset_done"], 3)
                pool.memset(av(reset)[:, :, 0:1], 0.0).then_inc(S["reset_done"], 1)
                m = 2
                for d in range(2):
                    sv = same[d][:].rearrange("p (c l) -> p c l", l=CHUNK)
                    sign = 1 if d == 0 else -1
                    pool.wait_ge(S["mask_done"], m)
                    pool.affine_select(out=sv, in_=sv, compare_op=ALU.is_ge, fill=0.0, base=0,
                                       pattern=[[sign * CHUNK, P // CHUNK], [sign, CHUNK]],
                                       channel_multiplier=-sign).then_inc(S["mask_done"], 1)
                    m += 1
                    pool.wait_ge(S["mask_done"], m)
                    pool.affine_select(out=sv, in_=sv, compare_op=ALU.is_ge, fill=0.0,
                                       base=0 if d == 0 else CHUNK - 1,
                                       pattern=[[-sign * CHUNK, P // CHUNK], [0, CHUNK]],
                                       channel_multiplier=sign).then_inc(S["mask_done"], 1)
                    m += 1
                pool.memset(v_by_chunk[:], 0.0).then_inc(S["vc_zero"], 1)

                def lo(q, j):
                    t.lo(pool, q * BODY + j, j % N_RAW, j % SPLIT)

                def turn(q, u, more):
                    if more:
                        for i in range(PER if more == 1 else PER - SPLIT):
                            lo(q, PER * (u + 1) + SPLIT + i)
                for j in range(PER + SPLIT):
                    lo(0, j)
                turns(pool, turn)

            @block.tensor
            def _(pe):
                def bank(x):
                    return t.psum[:, 4 + x]

                def tile(q, u, i, ks=range(KC)):
                    j = PER * u + i
                    t.product(pe, q * BODY + j, j % SPLIT, TOK if i < 3 else SEQ, t.h_hi, t.h_lo, ks)

                def to_tokens(h, x):
                    src = (vT, kk[0], kk[1])[x]
                    if x == 0:
                        pe.wait_ge(S["v_in"], h + 1)
                    else:
                        pe.wait_ge(S["kd_done"], h * 2 + x)
                    pe.wait_ge(S["tok_cp"], h * 3 + (x + 1))
                    for g in range(BLK):
                        last = pe.transpose(bank(g // 4)[:, (g % 4) * P:(g % 4 + 1) * P],
                                            src[:, g * P:(g + 1) * P], t.ident[:])
                    last.then_inc(S["tok_mm"], 1)

                def scores(h, d):
                    pe.wait_ge(S["m_done"], h * 4 + 2 * d + 2)
                    pe.wait_ge(S["prob_done"], h * 2 + d + 1)
                    for g in range(SEQ // P):
                        sl = slice(g * P, (g + 1) * P)
                        last = pe.matmul(bank(2)[:, sl], km[d][:, sl], qm[d][:, sl], start=True, stop=True)
                    last.then_inc(S["score_mm"], 1)

                def key_values(h, between):
                    pe.wait_ge(S["tok_cp"], h * 3 + 4)
                    pe.wait_ge(S["vc_done"], h + 1)
                    pe.wait_ge(S["prob_done"], h * 2 + 3)
                    pe.wait_ge(S["o_cp"], h + 1)
                    for x in range(len(KVG)):
                        if between and x:
                            for i, ks in between[x - 1]:
                                tile(*i, ks)
                        pe.wait_ge(S["kv_free"], h * len(KVG) + (x + 1))
                        for d in range(2):
                            g = BLOCK[d][x]
                            last = pe.matmul(bank(2 * d + x % 2), kd_tok[d][:, g],
                                             v_by_chunk[:, g].rearrange("p r x -> p (r x)"),
                                             start=True, stop=True)
                        last.then_inc(S["kv_mm"], 1)

                def output(h):
                    pe.wait_ge(S["st_done"], h * len(KV) + len(KV))
                    for d in range(2):
                        for g in range(SEQ // P):
                            sl = slice(g * P, (g + 1) * P)
                            pe.matmul(bank(3)[:, sl], v_tok[:, g], probs[d][:, sl],
                                      start=(d == 0 and g == 0), stop=False, skip_group_check=True)
                    pe.wait_ge(S["qd_done"], h * 2 + 2)
                    for d in range(2):
                        for c in range(XCH):
                            sl = slice(c * CHUNK, (c + 1) * CHUNK)
                            last = pe.matmul(bank(3)[:, sl], state[d][:, c], qd[d][:, sl], start=False,
                                             stop=(d == 1 and c == XCH - 1), skip_group_check=True)
                    last.then_inc(S["o_mm"], 1)

                def turn(q, u, more):
                    h = q * 2 + u
                    nxt = lambda i: tile(q, u + 1, i) if more else None
                    nxt(0)
                    to_tokens(h, 0)
                    nxt(1)
                    for d in range(2):
                        to_tokens(h, d + 1)
                        scores(h, d)
                    if more:
                        at = (q, u + 1)
                        tile(*at, 2, range(KC // 2))
                        steps = [(i, k) for i in range(2, 5) for k in range(KC)][KC // 2:-KC // 2]
                        parts = [steps[x * len(steps) // 5:(x + 1) * len(steps) // 5] for x in range(5)]
                        key_values(h, [[(at + (i,), [k]) for i, k in part] for part in parts])
                    else:
                        key_values(h, None)
                    output(h)
                    if more:
                        tile(*at, 4, range(KC // 2, KC))
                    pe.wait_ge(S["osq"], h + 1)
                    pe.matmul(bank(2), t.ones[:], osq, start=True, stop=True).then_inc(S["osum"], 1)
                for x in ("tok_cp", "prob_done", "o_cp"):
                    pe.sem_inc(S[x], 1)
                pe.sem_inc(S["kv_free"], 2)
                for i in range(PER):
                    tile(0, 0, i)
                turns(pe, turn)

            @block.scalar
            def _(act):
                def hi(q, j):
                    t.hi(act, q * BODY + j, j % N_RAW, j % SPLIT, q * (BODY // N_RAW) + j // N_RAW)

                def evac(q, u, i, more=1):
                    j = PER * u + i
                    h = q * 2 + u
                    t.wait_product(act, q * BODY + j)
                    T = TOK if i < 3 else SEQ
                    dst = (f[0][:], f[1][:], vT[:], qs[:], zs[:, u % 2])[i]
                    func = (ACT.Sigmoid, ACT.Sigmoid, ACT.Copy, ACT.Silu, ACT.Silu)[i]
                    name = ("f_in", "f_in", "v_in", "q_in", "z_in")[i]
                    act.activation(split_tokens(dst, T), t.acc(j % SPLIT, T), func).then_inc(S[name], 1)
                    act.wait_ge(S[name], h * 2 + (i + 1) if i < 2 else h + 1)
                    act.sem_inc(t.acc_free[j % SPLIT], 1)
                    if more == 1 or i < PER - SPLIT:
                        hi(q, j + SPLIT)

                def copy_tokens(h, x):
                    dst = (v_tok, kd_tok[0], kd_tok[1])[x]
                    act.wait_ge(S["tok_mm"], h * 3 + (x + 1))
                    for g0, g1 in ((0, 4), (4, BLK)):
                        last = act.activation(dst[:, g0:g1], t.psum[:, 4 + g0 // 4, 0:(g1 - g0) * P].rearrange(
                            "p (g x) -> p g x", x=P), ACT.Copy)
                    last.then_inc(S["tok_cp"], 1)

                def logs(h):
                    for d in range(2):
                        act.wait_ge(S["k_done"], h * 2 + (d + 1))
                        act.activation(f[d][:], f[d][:], ACT.Ln).then_inc(S["ln_done"], 1)

                def turn(q, u, more):
                    h = q * 2 + u
                    nxt = lambda i: evac(q, u + 1, i, more) if more else None
                    for d in range(2):
                        act.wait_ge(S["b_done"], h * 2 + (d + 1))
                        act.wait_ge(S["d2"], h * 2 + (d + 1))
                        act.activation(e[d][:], e[d][:], ACT.Exp).then_inc(S["d2_exp"], 1)
                        act.wait_ge(S["d1"], h * 2 + (d + 1))
                        act.activation(km[d][:], qm[d][:], ACT.Exp, scale=-1.0).then_inc(S["d1_exp"], 1)
                        act.wait_ge(S["d1_exp"], h * 4 + (2 * d + 1))
                        act.activation(qm[d][:], qm[d][:], ACT.Exp).then_inc(S["d1_exp"], 1)
                    for d in range(2):
                        act.activation(qd[d][:], b[d][:, 0:SEQ], ACT.Exp).then_inc(S["b_exp"], 1)
                        act.activation(dc[d][:].unsqueeze(2), av(b[d])[:, :, LAST[d]:LAST[d] + 1],
                                       ACT.Exp).then_inc(S["dc_done"], 1)
                    nxt(0)
                    copy_tokens(h, 0)
                    nxt(1)
                    copy_tokens(h, 1)
                    copy_tokens(h, 2)
                    if more:
                        logs(h + 1)
                    nxt(2)
                    act.wait_ge(S["qd_done"], h * 2 + 2)
                    nxt(3)
                    act.wait_ge(S["o_mm"], h + 1)
                    act.activation(o, t.psum[:, 7], ACT.Copy).then_inc(S["o_cp"], 1)
                    act.wait_ge(S["o_cp"], h + 2)
                    act.activation(osq, o, ACT.Square).then_inc(S["osq"], 1)
                    nxt(4)
                    act.wait_ge(S["osum"], h + 1)
                    act.activation(orn, t.psum[:, 6], ACT.Sqrt, bias=t.eps[:], scale=1.0 / P).then_inc(S["oroot"], 1)
                for j in range(SPLIT):
                    hi(0, j)
                for i in range(PER):
                    evac(0, 0, i)
                    if i == 1:
                        logs(0)
                turns(act, turn)

            @block.vector
            def _(dve):
                bcl = lambda ap, c: ap.to_broadcast([P, c, CHUNK])

                hs = lambda ap, h: ap[:, bass.ds(h, 1)]

                def decays(h):
                    for d in range(2):
                        dve.wait_ge(S["f_in"], h * 2 + (d + 1))
                        dve.tensor_scalar(f[d][:], f[d][:], hs(t.lb[:, 1, d], h), hs(t.lb[:, 0, d], h), ALU.mult,
                                          ALU.add).then_inc(S["f_done"], 1)
                        dve.wait_ge(S["f_done"], h * 2 + (d + 1))
                        dve.tensor_scalar(kk[d][:], f[d][:], -1.0, 1.0, ALU.mult, ALU.add).then_inc(S["k_done"], 1)
                    for d in range(2):
                        dve.wait_ge(S["ln_done"], h * 2 + (d + 1))
                        w = slice(None) if d == 0 else slice(None, None, -1)
                        dve.tensor_tensor_scan(b[d][:, w], reset[:], f[d][:, w], 0.0, ALU.mult,
                                               ALU.add).then_inc(S["b_done"], 1)

                def turn(q, u, more):
                    h = q * 2 + u
                    dve.wait_ge(S["q_in"], h + 1)
                    for d in range(2):
                        dve.wait_ge(S["b_done"], h * 2 + (d + 1))
                        dve.tensor_tensor(av(e[d]), bcl(av(b[d])[:, :, LAST[d]:LAST[d] + 1], NCH), av(b[d]),
                                          ALU.subtract).then_inc(S["d2"], 1)
                        dve.tensor_tensor(xv(qm[d]), xv(b[d]), bcl(xv(b[d])[:, :, MID[d]:MID[d] + 1], XCH),
                                          ALU.subtract).then_inc(S["d1"], 1)
                    for d in range(2):
                        dve.wait_ge(S["d1_exp"], h * 4 + 2 * d + 2)
                        dve.tensor_tensor(km[d][:], km[d][:], kk[d][:, 0:SEQ], ALU.mult).then_inc(S["m_done"], 1)
                        dve.tensor_tensor(qm[d][:], qm[d][:], qs[:], ALU.mult).then_inc(S["m_done"], 1)
                        dve.wait_ge(S["d2_exp"], h * 2 + d + 1)
                        dve.wait_ge(S["m_done"], h * 4 + 2 * d + 1)
                        dve.tensor_tensor(kk[d][:], kk[d][:], e[d][:], ALU.mult).then_inc(S["kd_done"], 1)
                    dve.wait_ge(S["tok_cp"], h * 3 + 2)
                    for r in range(ROWS):
                        rows = slice(r * CHUNK, (r + 1) * CHUNK)
                        last = dve.tensor_copy(v_by_chunk[rows, :, r], v_tok[rows])
                    last.then_inc(S["vc_done"], 1)
                    for d in range(2):
                        dve.wait_ge(S["b_exp"], h * 2 + d + 1)
                        dve.tensor_tensor(qd[d][:], qd[d][:], qs[:], ALU.mult).then_inc(S["qd_done"], 1)
                    dve.wait_ge(S["mask_done"], 6)
                    for d in range(2):
                        dve.wait_ge(S["score_mm"], h * 2 + d + 1)
                        t.settle(dve)
                        dve.copy_predicated(probs[d][:].rearrange("p (g l) -> p g l", l=P),
                                            same[d][:].bitcast(U32).unsqueeze(1).to_broadcast([P, SEQ // P, P]),
                                            t.psum[:, 6].rearrange("p (g l) -> p g l", l=P)).then_inc(S["prob_done"], 1)
                    dve.wait_ge(S["dc_done"], h * 2 + 2)
                    if more:
                        dve.wait_ge(S["tok_mm"], h * 3 + 3)
                        decays(h + 1)
                    at = 0
                    for x, grp in enumerate(KVG):
                        dve.wait_ge(S["kv_mm"], h * len(KVG) + x + 1)
                        for s, d in grp:
                            c = ORDER[d][s]
                            r = c % ROWS
                            kv = t.psum[:, 4 + 2 * d + x % 2, r * P:(r + 1) * P]
                            dst = state[d][:, ORDER[d][max(s + 1, CCH)]]
                            if s == 0:
                                ins = dve.tensor_copy(dst, kv)
                            else:
                                dve.wait_ge(S["st_done"], h * len(KV) + at - 1)
                                ins = dve.scalar_tensor_tensor(
                                    out=dst, in0=state[d][:, ORDER[d][max(s, CCH)]], scalar=dc[d][:, c:c + 1],
                                    in1=kv, op0=ALU.mult, op1=ALU.add)
                            ins.then_inc(S["st_done"], 1)
                            at += 1
                        dve.wait_ge(S["st_done"], h * len(KV) + at)
                        dve.sem_inc(S["kv_free"], 1)
                    dve.wait_ge(S["oroot"], h + 1)
                    dve.reciprocal(orn, orn).then_inc(S["on"], 1)
                    dve.wait_ge(S["on"], h * 2 + 1)
                    dve.tensor_tensor(ony, o, orn, ALU.mult).then_inc(S["on"], 1)
                    dve.wait_ge(S["on"], h * 2 + 2)
                    dve.wait_ge(S["z_in"], h + 1)
                    dve.scalar_tensor_tensor(out=y[:, bass.ds(h, 1)].rearrange("p a n -> p (a n)"), in0=ony,
                                             scalar=hs(t.gains[:, 5], h), in1=zs[:, u], op0=ALU.mult,
                                             op1=ALU.mult).then_inc(S["y_done"], 1)
                    dve.wait_ge(S["y_done"], h + 1)
                dve.wait_ge(S["reset_done"], 4)
                dve.wait_ge(S["vc_zero"], 1)
                decays(0)
                turns(dve, turn)
        t.end_stage(n, N_RAW)


def stage_split(t, y):
    nc = t.nc
    hi_done, lo_done = t.sem("y_hi_done"), t.sem("y_lo_done")
    with nc.Block() as block:

        @block.scalar
        def _(act):
            for k in range(KC):
                act.activation(t.h_hi[:, k, 0:SEQ], y[:, k], ACT.Copy).then_inc(hi_done, 1)

        @block.vector
        def _(dve):
            for k in range(KC):
                dve.wait_ge(hi_done, k + 1)
                dve.tensor_tensor(t.h_lo[:, k, 0:SEQ], y[:, k], t.h_hi[:, k, 0:SEQ].bitcast(F32),
                                  ALU.subtract).then_inc(lo_done, 1)
            dve.wait_ge(lo_done, KC)


def hybrid_trunk(nc, a):
    with ExitStack() as ctx:
        t = Trunk(nc, ctx, a)
        g_dram = [nc.dram_tensor(f"gates{i}", [GROUPS, P, T // STAGE_T, QUAD * STAGE_T], F32, kind="Internal").ap()
                  for i, T in enumerate((TOK, SEQ))]
        act_dram = [nc.dram_tensor(f"acts{i}", [AHEAD[i] * T // P, P, T], F32, kind="Internal").ap()
                    for i, T in enumerate((TOK, SEQ))]
        stage_setup(t)
        for layer, tokens in enumerate((TOK, SEQ)):
            stage_norm(t, layer, 0, TOK)
            with ExitStack() as mix:
                if layer == 0:
                    y_hi = mix.enter_context(nc.sbuf_tensor("y_hi", [P, KC, TOK], F32R))
                    y_lo = mix.enter_context(nc.sbuf_tensor("y_lo", [P, KC, TOK], F32R))
                    stage_conv(t, y_hi, y_lo)
                    stage_mix_out(t, layer, "conv_w_out", tokens, y_hi, y_lo)
                else:
                    y = mix.enter_context(nc.sbuf_tensor("y_heads", [P, KC, SEQ], F32))
                    stage_hgrn(t, y)
                    stage_split(t, y)
                    stage_mix_out(t, layer, "hgrn_w_out", tokens, t.h_hi, t.h_lo)
            stage_norm(t, layer, 1, tokens)
            with ExitStack() as pick:
                top = pick.enter_context(nc.sbuf_tensor(f"top{layer}", [P, tokens // P, LISTS, TOPK], F32))
                top_i = pick.enter_context(nc.sbuf_tensor(f"top_i{layer}", [P, tokens // P, LISTS, TOPK], U32))
                stage_rank(t, layer, tokens, top, top_i)
                stage_gates(t, layer, tokens, top, top_i, g_dram[layer], act_dram[layer])
            stage_experts(t, layer, tokens, g_dram[layer], act_dram[layer])
            if layer == 0:
                t.retire()
        stage_norm(t, 1, 2, SEQ)


def kernel(**inputs):
    import numpy as np
    import concourse.bacc as bacc
    from concourse.bass_utils import run_bass_kernel_spmd

    i = {k: np.asarray(v) for k, v in inputs.items()}

    def cols(v):
        v = v.reshape(v.shape[:-1] + (-1, P))
        return np.moveaxis(v, -1, 0)

    def tiles(w):
        k, m = w.shape
        return w.reshape(k // P, P, m // P, P).transpose(2, 1, 0, 3).reshape(m // P, P, k)

    def grouped(w, order):
        tl = tiles(w).reshape(-1, KC, P, D)
        return tl[order].transpose(1, 0, 2, 3).reshape(-1, P, D)

    send = {
        "x": i["x"][0].T.reshape(KC, P, SEQ).transpose(1, 0, 2),
        "ctx": i["ctx"][0].T.reshape(KC, P, CTX).transpose(1, 0, 2),
        "cond": np.stack([cols(i["c"][0]), cols(i["c_ctx"])], axis=-1),
        "ada_w": i["ada_w"][0].reshape(KC, P, 12, 512).transpose(2, 1, 0, 3),
        "ada_w1": i["ada_w"][1].T.reshape(48, P, D),
        "cond_rows": np.broadcast_to(np.stack([i["c"][0].reshape(D), i["c_ctx"].reshape(D)]), (P, 2, D)),
        "ada_b": cols(i["ada_b"]),
        "gains": cols(np.stack([i["norm1_g"][0], i["norm1_g"][1], i["norm2_g"][0], i["norm2_g"][1],
                                i["final_g"], i["hgrn_norm_g"][0]])),
        "hgrn_lb": cols(i["hgrn_lb"]),
        "conv_w_in": grouped(i["conv_w_in"][0], [1, 2, 0]),
        "conv_k": cols(i["conv_k"][0]).transpose(0, 2, 1),
        "conv_w_out": tiles(i["conv_w_out"][0]),
        "hgrn_w_in": grouped(i["hgrn_w_in"][0], [2, 3, 1, 0, 4]),
        "hgrn_w_out": tiles(i["hgrn_w_out"][0]),
        "peer_keys": i["peer_keys"].reshape(2, LISTS, NKEYS, P).transpose(0, 3, 1, 2),
    }
    for n in range(2):
        send[f"peer_w_q{n}"] = tiles(i["peer_w_q"][n])
        u = i["peer_u"][n].reshape(NKEYS, NKEYS, KC, P)
        send[f"peer_u{n}"] = u.transpose(1, 3, 2, 0).reshape(NKEYS, P, D)
        send[f"peer_v{n}"] = i["peer_v"][n].reshape(NKEYS, NKEYS, D).transpose(1, 0, 2)
    send = {k: np.ascontiguousarray(v) for k, v in send.items()}

    nc = bacc.Bacc("TRN2", target_bir_lowering=False, num_devices=1)
    a = {k: nc.dram_tensor("in_" + k, v.shape, mybir.dt.from_np(v.dtype), kind="ExternalInput").ap()
         for k, v in send.items()}
    a["out"] = nc.dram_tensor("out_x", (P, KC, SEQ), F32, kind="ExternalOutput").ap()
    hybrid_trunk(nc, a)
    r = run_bass_kernel_spmd(nc, [{"in_" + k: v for k, v in send.items()}], core_ids=[0])
    out = r.results[0]["out_x"]
    return np.ascontiguousarray(out.transpose(2, 1, 0)).reshape(1, SEQ, D)
```
